# Optimizing a Trainium2 kernel written in Bass

```python
import numpy as np
import jax
import jax.numpy as jnp
from jax import lax

D_MODEL = 1024
BATCH = 1
SEQ = 256
DEPTH = 2

CONV_CH = D_MODEL // 2
CONV_WIDTH = 31
NSA_HEADS = 8
NSA_KV_HEADS = 2
HEAD_DIM = (D_MODEL // 2) // NSA_HEADS
CMP_BLOCK = 32
CMP_STRIDE = 16
CMP_HIDDEN = 256
SEL_BLOCK = 64
SEL_TOP_N = 16
WINDOW = 512
Q_BLOCK = 128
FORCE_SCORE = 1e4
SHORT_CONV_WIDTH = 3
MEM_LEN = 256
XA_HEADS = 4
XA_HEAD_DIM = D_MODEL // XA_HEADS
N_GROUPS = 4
EXPERTS_PER_GROUP = 8
N_EXPERTS = N_GROUPS * EXPERTS_PER_GROUP
EXPERT_HIDDEN = D_MODEL // 2
EXPERT_TOP_K = 2
DISPATCH_ROWS = 256
DN_ALPHA = (2 * DEPTH) ** 0.25
DN_BETA = (8 * DEPTH) ** -0.25
LN_EPS = 1e-5
NEG_INF = -1e30

KV_COLS = NSA_KV_HEADS * HEAD_DIM
EVEN_SPLIT_SIZES = (CONV_CH, CONV_CH, NSA_HEADS * HEAD_DIM, KV_COLS, KV_COLS, KV_COLS, KV_COLS, KV_COLS, KV_COLS, 3 * NSA_HEADS)
EVEN_IN_COLS = sum(EVEN_SPLIT_SIZES)

kernel_name = 'hybrid_conformer_nsa_shortconv_hmoe'

def layer_norm(x, g, b):
    xf = x.astype(jnp.float32)
    mu = jnp.mean(xf, -1, keepdims=True)
    var = jnp.mean(jnp.square(xf - mu), -1, keepdims=True)
    y = (xf - mu) * lax.rsqrt(var + LN_EPS)
    return (y * g.astype(jnp.float32) + b.astype(jnp.float32)).astype(x.dtype)

def causal_depthwise_conv(u, w):
    k = w.shape[0]
    return lax.conv_general_dilated(u, w[:, None, :].astype(u.dtype), window_strides=(1,), padding=((k - 1, 0),), dimension_numbers=('NWC', 'WIO', 'NWC'), feature_group_count=u.shape[-1])

def masked_softmax(s, mask):
    p = jax.nn.softmax(jnp.where(mask, s, NEG_INF), axis=-1)
    return jnp.where(mask, p, 0.0)

def compress_blocks(kv, pe, w1, w2):
    b, s, g, dh = kv.shape
    n_cmp = (s - CMP_BLOCK) // CMP_STRIDE + 1
    idx = np.arange(n_cmp)[:, None] * CMP_STRIDE + np.arange(CMP_BLOCK)[None, :]
    blocks = kv[:, idx] + pe[None, None, :, None, :].astype(kv.dtype)
    blocks = jnp.transpose(blocks, (0, 1, 3, 2, 4)).reshape(b, n_cmp, g, CMP_BLOCK * dh)
    return jax.nn.gelu(blocks @ w1) @ w2

def cmp_to_sel_matrix(n_cmp, n_sel):
    c0 = np.arange(n_cmp) * CMP_STRIDE
    s0 = np.arange(n_sel) * SEL_BLOCK
    ov = np.minimum(c0[:, None] + CMP_BLOCK, s0[None, :] + SEL_BLOCK) - np.maximum(c0[:, None], s0[None, :])
    return (np.clip(ov, 0, None) / CMP_BLOCK).astype(np.float32)

def nsa_attention(q, k_cmp, v_cmp, k_sel, v_sel, k_win, v_win, gates):
    b, s, h, dh = q.shape
    g = NSA_KV_HEADS
    hg = h // g
    n_cmp = k_cmp.shape[1]
    n_sel = s // SEL_BLOCK
    top_n = min(SEL_TOP_N, n_sel)
    scale = dh ** -0.5
    m_sel = jnp.asarray(cmp_to_sel_matrix(n_cmp, n_sel))
    cmp_end = jnp.arange(n_cmp) * CMP_STRIDE + CMP_BLOCK - 1
    blk_ids = jnp.arange(n_sel)
    ks_blk = k_sel.reshape(b, n_sel, SEL_BLOCK, g, dh).transpose(0, 3, 1, 2, 4)
    vs_blk = v_sel.reshape(b, n_sel, SEL_BLOCK, g, dh).transpose(0, 3, 1, 2, 4)
    zpad = jnp.zeros((b, WINDOW, g, dh), k_win.dtype)
    kw_pad = jnp.concatenate([zpad, k_win], axis=1)
    vw_pad = jnp.concatenate([zpad, v_win], axis=1)
    bi = jnp.arange(b)[:, None, None, None]
    gi = jnp.arange(g)[None, :, None, None]
    f32 = jnp.float32

    def query_block(c):
        q0 = c * Q_BLOCK
        t = q0 + jnp.arange(Q_BLOCK)
        qc = lax.dynamic_slice_in_dim(q, q0, Q_BLOCK, axis=1).reshape(b, Q_BLOCK, g, hg, dh)
        gc = lax.dynamic_slice_in_dim(gates, q0, Q_BLOCK, axis=1).reshape(b, Q_BLOCK, g, hg, 3)
        s_c = jnp.einsum('bqghd,bngd->bghqn', qc, k_cmp, preferred_element_type=f32) * scale
        p_c = masked_softmax(s_c, cmp_end[None, :] <= t[:, None])
        o_c = jnp.einsum('bghqn,bngd->bqghd', p_c.astype(v_cmp.dtype), v_cmp)
        imp = jnp.einsum('bghqn,nm->bgqm', p_c, m_sel)
        cur = t // SEL_BLOCK
        forced = (blk_ids[None, :] == 0) | (blk_ids[None, :] == cur[:, None]) | (blk_ids[None, :] == cur[:, None] - 1)
        score = jnp.where(forced, FORCE_SCORE, imp)
        score = jnp.where(blk_ids[None, :] * SEL_BLOCK <= t[:, None], score, NEG_INF)
        top_score, top_idx = lax.top_k(score, top_n)
        blk_ok = top_score > 0.5 * NEG_INF
        k_g = ks_blk[bi, gi, top_idx]
        v_g = vs_blk[bi, gi, top_idx]
        s_s = jnp.einsum('bqghd,bgqnld->bghqnl', qc, k_g, preferred_element_type=f32) * scale
        key_pos = top_idx[..., None] * SEL_BLOCK + jnp.arange(SEL_BLOCK)
        mask_s = (blk_ok[..., None] & (key_pos <= t[None, None, :, None, None]))[:, :, None]
        p_s = masked_softmax(s_s.reshape(b, g, hg, Q_BLOCK, top_n * SEL_BLOCK), mask_s.reshape(b, g, 1, Q_BLOCK, top_n * SEL_BLOCK))
        p_s = p_s.reshape(b, g, hg, Q_BLOCK, top_n, SEL_BLOCK).astype(v_g.dtype)
        o_s = jnp.einsum('bghqnl,bgqnld->bqghd', p_s, v_g)
        kw = lax.dynamic_slice_in_dim(kw_pad, q0, WINDOW + Q_BLOCK, axis=1)
        vw = lax.dynamic_slice_in_dim(vw_pad, q0, WINDOW + Q_BLOCK, axis=1)
        kpos = q0 - WINDOW + jnp.arange(WINDOW + Q_BLOCK)
        mask_w = (kpos[None, :] <= t[:, None]) & (kpos[None, :] > t[:, None] - WINDOW) & (kpos[None, :] >= 0)
        s_w = jnp.einsum('bqghd,bkgd->bghqk', qc, kw, preferred_element_type=f32) * scale
        p_w = masked_softmax(s_w, mask_w)
        o_w = jnp.einsum('bghqk,bkgd->bqghd', p_w.astype(vw.dtype), vw)
        o = gc[..., 0:1] * o_c + gc[..., 1:2] * o_s + gc[..., 2:3] * o_w
        return o.reshape(b, Q_BLOCK, h * dh)

    out = lax.map(query_block, jnp.arange(s // Q_BLOCK))
    return jnp.transpose(out, (1, 0, 2, 3)).reshape(b, s, h * dh)

def even_mixer(x, w_in, conv_w, conv_b, cn_g, cn_b, pe_k, w1_k, w2_k, pe_v, w1_v, w2_v, w_out):
    b, s, _ = x.shape
    split_pts = np.cumsum(EVEN_SPLIT_SIZES)[:-1].tolist()
    a_val, a_gate, q, kc, vc, ks, vs, kw, vw, gl = jnp.split(x @ w_in, split_pts, axis=-1)
    a = a_val * jax.nn.sigmoid(a_gate)
    a = causal_depthwise_conv(a, conv_w) + conv_b.astype(a.dtype)
    a = jax.nn.silu(layer_norm(a, cn_g, cn_b))
    kvs = lambda u: u.reshape(b, s, NSA_KV_HEADS, HEAD_DIM)
    k_cmp = compress_blocks(kvs(kc), pe_k, w1_k, w2_k)
    v_cmp = compress_blocks(kvs(vc), pe_v, w1_v, w2_v)
    gates = jax.nn.sigmoid(gl).reshape(b, s, NSA_HEADS, 3)
    o = nsa_attention(q.reshape(b, s, NSA_HEADS, HEAD_DIM), k_cmp, v_cmp, kvs(ks), kvs(vs), kvs(kw), kvs(vw), gates)
    return jnp.concatenate([a, o], axis=-1) @ w_out

def odd_mixer(x, w_in, conv_w, w_out):
    gate_b, gate_c, h = jnp.split(x @ w_in, 3, axis=-1)
    return (gate_b * causal_depthwise_conv(gate_c * h, conv_w)) @ w_out

def memory_cross_attention(x, mem_k, mem_v, wq, wo):
    b, s, d = x.shape
    q = (x @ wq).reshape(b, s, XA_HEADS, XA_HEAD_DIM)
    sc = jnp.einsum('bshd,bmhd->bhsm', q, mem_k, preferred_element_type=jnp.float32) * XA_HEAD_DIM ** -0.5
    p = jax.nn.softmax(sc, axis=-1).astype(x.dtype)
    return jnp.einsum('bhsm,bmhd->bshd', p, mem_v).reshape(b, s, d) @ wo

def hierarchical_moe(x, wg, bg, we, be, w1, w3, w2):
    b, s, d = x.shape
    n_tok = b * s
    xt = x.reshape(n_tok, d)
    xf = xt.astype(jnp.float32)
    g_logits = xf @ wg.astype(jnp.float32) + bg.astype(jnp.float32)
    g_star = jnp.argmax(g_logits, axis=-1)
    p_group = jnp.take_along_axis(jax.nn.softmax(g_logits, axis=-1), g_star[:, None], axis=-1)
    e_logits = jnp.einsum('td,dge->tge', xf, we.astype(jnp.float32)) + be.astype(jnp.float32)
    e_logits = jnp.take_along_axis(e_logits, g_star[:, None, None], axis=1)[:, 0]
    top_val, top_idx = lax.top_k(e_logits, EXPERT_TOP_K)
    gate = (p_group * jax.nn.softmax(top_val, axis=-1)).reshape(-1)
    expert = (g_star[:, None] * EXPERTS_PER_GROUP + top_idx).reshape(-1).astype(jnp.int32)
    token = jnp.repeat(jnp.arange(n_tok, dtype=jnp.int32), EXPERT_TOP_K)
    n_assign = n_tok * EXPERT_TOP_K
    n_blocks = n_assign // DISPATCH_ROWS + N_EXPERTS + 1
    order = jnp.argsort(expert)
    e_sorted = expert[order]
    tok_sorted = token[order]
    gate_sorted = gate[order]
    counts = jnp.bincount(expert, length=N_EXPERTS)
    start = jnp.cumsum(counts) - counts
    padded = (counts + DISPATCH_ROWS - 1) // DISPATCH_ROWS * DISPATCH_ROWS
    pad_end = jnp.cumsum(padded)
    pad_start = pad_end - padded
    dest = pad_start[e_sorted] + jnp.arange(n_assign) - start[e_sorted]
    x_disp = jnp.zeros((n_blocks * DISPATCH_ROWS, d), x.dtype).at[dest].set(xt[tok_sorted])
    block_expert = jnp.minimum(jnp.searchsorted(pad_end, jnp.arange(n_blocks) * DISPATCH_ROWS, side='right'), N_EXPERTS - 1)

    def expert_block(args):
        xb, e = args
        return (jax.nn.silu(xb @ w1[e]) * (xb @ w3[e])) @ w2[e]

    y_disp = lax.map(expert_block, (x_disp.reshape(n_blocks, DISPATCH_ROWS, d), block_expert))
    y = y_disp.reshape(-1, d)[dest] * gate_sorted[:, None].astype(x.dtype)
    return jax.ops.segment_sum(y, tok_sorted, num_segments=n_tok).reshape(b, s, d)

def setup_inputs(seed: int = 0) -> dict:
    key = jax.random.key(seed)
    keys = list(jax.random.split(key, 40))

    def nrm(shape, scale):
        return jax.random.normal(keys.pop(), shape, jnp.float32) * scale

    def gain(shape):
        return 1.0 + nrm(shape, 0.02)

    d = D_MODEL
    ne = (DEPTH + 1) // 2
    no = DEPTH // 2
    return {
        'x': nrm((BATCH, SEQ, d), 1.0),
        'mem': nrm((BATCH, MEM_LEN, d), 1.0),
        'mem_wk': nrm((d, d), d ** -0.5),
        'mem_wv': nrm((d, d), d ** -0.5),
        'ev_w_in': nrm((ne, d, EVEN_IN_COLS), d ** -0.5),
        'ev_conv_w': nrm((ne, CONV_WIDTH, CONV_CH), CONV_WIDTH ** -0.5),
        'ev_conv_b': nrm((ne, CONV_CH), 0.02),
        'ev_cnorm_g': gain((ne, CONV_CH)),
        'ev_cnorm_b': nrm((ne, CONV_CH), 0.02),
        'ev_cmp_pe_k': nrm((ne, CMP_BLOCK, HEAD_DIM), 0.02),
        'ev_cmp_w1_k': nrm((ne, CMP_BLOCK * HEAD_DIM, CMP_HIDDEN), (CMP_BLOCK * HEAD_DIM) ** -0.5),
        'ev_cmp_w2_k': nrm((ne, CMP_HIDDEN, HEAD_DIM), CMP_HIDDEN ** -0.5),
        'ev_cmp_pe_v': nrm((ne, CMP_BLOCK, HEAD_DIM), 0.02),
        'ev_cmp_w1_v': nrm((ne, CMP_BLOCK * HEAD_DIM, CMP_HIDDEN), (CMP_BLOCK * HEAD_DIM) ** -0.5),
        'ev_cmp_w2_v': nrm((ne, CMP_HIDDEN, HEAD_DIM), CMP_HIDDEN ** -0.5),
        'ev_w_out': nrm((ne, CONV_CH + NSA_HEADS * HEAD_DIM, d), (CONV_CH + NSA_HEADS * HEAD_DIM) ** -0.5 * DN_BETA),
        'od_w_in': nrm((no, d, 3 * d), d ** -0.5),
        'od_conv_w': nrm((no, SHORT_CONV_WIDTH, d), SHORT_CONV_WIDTH ** -0.5),
        'od_w_out': nrm((no, d, d), d ** -0.5 * DN_BETA),
        'ln_mix_g': gain((DEPTH, d)),
        'ln_mix_b': nrm((DEPTH, d), 0.02),
        'xa_wq': nrm((DEPTH, d, d), d ** -0.5),
        'xa_wo': nrm((DEPTH, d, d), d ** -0.5 * DN_BETA),
        'ln_xa_g': gain((DEPTH, d)),
        'ln_xa_b': nrm((DEPTH, d), 0.02),
        'moe_wg': nrm((DEPTH, d, N_GROUPS), d ** -0.5),
        'moe_bg': nrm((DEPTH, N_GROUPS), 0.01),
        'moe_we': nrm((DEPTH, d, N_GROUPS, EXPERTS_PER_GROUP), d ** -0.5),
        'moe_be': nrm((DEPTH, N_GROUPS, EXPERTS_PER_GROUP), 0.01),
        'moe_w1': nrm((DEPTH, N_EXPERTS, d, EXPERT_HIDDEN), d ** -0.5),
        'moe_w3': nrm((DEPTH, N_EXPERTS, d, EXPERT_HIDDEN), d ** -0.5),
        'moe_w2': nrm((DEPTH, N_EXPERTS, EXPERT_HIDDEN, d), EXPERT_HIDDEN ** -0.5 * DN_BETA),
        'ln_ffn_g': gain((DEPTH, d)),
        'ln_ffn_b': nrm((DEPTH, d), 0.02),
    }

def reference(x, mem, mem_wk, mem_wv, ev_w_in, ev_conv_w, ev_conv_b, ev_cnorm_g, ev_cnorm_b, ev_cmp_pe_k, ev_cmp_w1_k, ev_cmp_w2_k, ev_cmp_pe_v, ev_cmp_w1_v, ev_cmp_w2_v, ev_w_out, od_w_in, od_conv_w, od_w_out, ln_mix_g, ln_mix_b, xa_wq, xa_wo, ln_xa_g, ln_xa_b, moe_wg, moe_bg, moe_we, moe_be, moe_w1, moe_w3, moe_w2, ln_ffn_g, ln_ffn_b):
    b = x.shape[0]
    m_len = mem.shape[1]
    mem_k = (mem @ mem_wk).reshape(b, m_len, XA_HEADS, XA_HEAD_DIM)
    mem_v = (mem @ mem_wv).reshape(b, m_len, XA_HEADS, XA_HEAD_DIM)
    for layer in range(DEPTH):
        i = layer // 2
        if layer % 2 == 0:
            mix = even_mixer(x, ev_w_in[i], ev_conv_w[i], ev_conv_b[i], ev_cnorm_g[i], ev_cnorm_b[i], ev_cmp_pe_k[i], ev_cmp_w1_k[i], ev_cmp_w2_k[i], ev_cmp_pe_v[i], ev_cmp_w1_v[i], ev_cmp_w2_v[i], ev_w_out[i])
        else:
            mix = odd_mixer(x, od_w_in[i], od_conv_w[i], od_w_out[i])
        x = layer_norm(DN_ALPHA * x + mix, ln_mix_g[layer], ln_mix_b[layer])
        x = layer_norm(DN_ALPHA * x + memory_cross_attention(x, mem_k, mem_v, xa_wq[layer], xa_wo[layer]), ln_xa_g[layer], ln_xa_b[layer])
        x = layer_norm(DN_ALPHA * x + hierarchical_moe(x, moe_wg[layer], moe_bg[layer], moe_we[layer], moe_be[layer], moe_w1[layer], moe_w3[layer], moe_w2[layer]), ln_ffn_g[layer], ln_ffn_b[layer])
    return x


_drawn_inputs = setup_inputs


def setup_inputs(seed=0):
    import zlib

    import numpy as np

    out = dict(_drawn_inputs(seed))
    spreads = {}
    factors = {'ev_conv_b': 5.165,
     'ev_cnorm_g': 7.81,
     'ev_cnorm_b': 6.716,
     'ev_cmp_pe_k': 64.0,
     'ev_cmp_w2_k': 2.84,
     'ev_cmp_pe_v': 35.362,
     'moe_bg': 8.0,
     'moe_be': 6.695}
    for name, (base, spread) in spreads.items():
        noise = np.random.default_rng([zlib.crc32(name.encode()), seed]).standard_normal(out[name].shape)
        drawn = base * np.exp(spread * noise) if base else spread * noise
        out[name] = jnp.asarray(drawn.astype(out[name].dtype))
    for name, factor in factors.items():
        out[name] = (out[name] * factor).astype(out[name].dtype)
    return out
```

```python
from contextlib import ExitStack

import concourse.bass as bass
from concourse import mybir

F32 = mybir.dt.float32
BF16 = mybir.dt.bfloat16
U32 = mybir.dt.uint32
I32 = mybir.dt.int32
ACT = mybir.ActivationFunctionType
ALU = mybir.AluOpType
AX = mybir.AxisListType.X

P = 128
D = 1024
S = 256
TT = S // P
KC = D // P
DEPTH = 2
CONV_CH = D // 2
CC = CONV_CH // P
TAPS = 31
PAD = TAPS - 1
HEADS = 8
HD = (D // 2) // HEADS
CMP_STRIDE = 16
NCMP = (S - 32) // CMP_STRIDE + 1
XH = 4
NG = 4
EPG = 8
NE = NG * EPG
CAP = 64
PAIRS = NE // 2
PASSES = S // CAP
RING = 6
ALPHA = (2 * DEPTH) ** 0.25
EPS = 1e-5
NEG = -1e30
GELU_A = 0.044715
GELU_B = 0.7978845608028654
LN_COUNT = 3 * DEPTH
C_CB, C_CG, C_CN, C_OD, C_PK, C_PV, C_ALL = 0, 4, 8, 12, 36, 52, 68


class Steps:

    def __init__(self, eng, sem):
        self.eng, self.sem, self.n = eng, sem, 0

    def mark(self, ins):
        ins.then_inc(self.sem, 1)
        self.n += 1
        return self.n

    def wait(self, n=None):
        self.eng.wait_ge(self.sem, self.n if n is None else n)

    def do(self, ins):
        self.mark(ins)
        self.wait()


def program(nc, T, out):
    ctx = ExitStack()
    with ctx:
        def sb(name, shape, dt=F32):
            return ctx.enter_context(nc.sbuf_tensor(name, shape, dt))

        def sem(name):
            return ctx.enter_context(nc.semaphore(name))

        ring = sb("ring", [P, RING, 4096])
        x = sb("x", [P, TT, D])
        xT = sb("xT", [P, KC, S])
        memT = sb("memT", [P, KC, S])
        qxT = memT
        oT = sb("oT", [P, KC, S])
        mem_kT = sb("mem_kT", [P, KC, S])
        mem_v = sb("mem_v", [P, TT, D])
        gb = sb("gb", [P, 2, D])
        qT = sb("qT", [P, CC, S])
        aT = sb("aT", [P, CC, PAD + S])
        kT = sb("kT", [P, 2, 2 * S])
        xgT = kT[:, :, :].rearrange("p a b -> p (a b)").rearrange("p (k s) -> p k s", k=KC)
        blocks = sb("blocks", [P, 2, 16, 2, NCMP])
        v_sb = sb("v_sb", [P, TT, 2, P])
        prob = sb("prob", [P, 2, 2, 2 * S])
        probT = sb("probT", [P, 2, 2, TT, S])
        pc = sb("pc", [P, TT, HEADS, 16])
        pcT = sb("pcT", [16, 2, S])
        k_cmpT = sb("k_cmpT", [P, 2, 16])
        v_cmp = sb("v_cmp", [16, 2, HD])
        ghid = sb("ghid", [P, 4, 32])
        gtmp = sb("gtmp", [P, 4, 32])
        w2c = sb("w2c", [P, 2, 2, HD])
        gates = sb("gates", [P, TT, 24])
        stat = sb("stat", [P, 64])
        scr = sb("scr", [P, 2, S])
        ident = sb("ident", [P, P])
        tri = sb("tri", [P, P])
        ones = sb("ones", [P, P])
        onesc = sb("onesc", [P, P])
        causal = sb("causal", [P, P])
        cmask = sb("cmask", [P, TT, 16])
        cbias = sb("cbias", [P, TT, 16])
        zero16 = sb("zero16", [P, 512], BF16)
        half = sb("half", [P, S])
        iota = sb("iota", [P, CAP])
        rows1 = sb("rows1", [P, P])
        rows2 = sb("rows2", [C_ALL, P])
        cw = sb("cw", [P, TAPS * CC])
        cols = sb("cols", [P, C_ALL])
        lngT = sb("lngT", [P, LN_COUNT, 2, KC])
        wr = sb("wr", [P, DEPTH, KC, NG + NE])
        rbias = sb("rbias", [P, DEPTH, NG + NE])
        lg = sb("lg", [P, TT, NG + NE])
        g8 = sb("g8", [P, TT, 8])
        top = sb("top", [P, TT, 2, 8])
        topi = sb("topi", [P, TT, 2, 8], U32)
        topf = sb("topf", [P, TT, 2, 8])
        ohg = sb("ohg", [P, TT, NG])
        esel = sb("esel", [P, TT, 8])
        etmp = sb("etmp", [P, TT, NG, EPG])
        e01 = sb("e01", [P, 2, TT, EPG])
        rs = sb("rs", [P, 8, TT])
        mask = sb("mask", [P, TT, NE])
        place = sb("place", [P, TT, NE + 2])
        gate = sb("gate", [P, TT, NE + 2])
        most = sb("most", [P, 2])
        mosti = sb("mosti", [P, 1], I32)
        probT_flat = probT[:, :, :, :, :].rearrange("p a b k s -> p (a b k s)")
        prob_flat = prob[:, :, :, :].rearrange("p a t s -> p (a t s)")
        disp = probT_flat[:, 0:256].rearrange("p (t e s) -> p t e s", t=TT, e=2)
        dispg = probT_flat[:, 256:768].rearrange("p (e t a s) -> p e t a s", e=2, t=TT, a=2)
        hid = probT_flat[:, 768:1024]
        hidT = probT_flat[:, 1024:1280].rearrange("p (c s) -> p c s", c=2)
        u = probT_flat[:, 1280:1536]
        comb = prob_flat[:, 0:512].rearrange("p (e s) -> p e s", e=2)
        th = prob_flat[:, 512:768]
        y = prob_flat[:, 1024:2048].rearrange("p (e n) -> p e n", e=2)
        bn = sb("bn", [P, TT, 2, 6])
        mv = sb("mv", [P, TT, 2])
        rstd = sb("rstd", [P, TT, 1])
        esum = sb("esum", [P, TT, NG])
        vare = sb("vare", [P, TT, 1])

        banks = [ctx.enter_context(nc.psum_tensor(f"bank{i}", [P, 512], F32)) for i in range(8)]

        loaded = [sem(f"loaded{i}") for i in range(RING)]
        weights_used = sem("weights_used")
        bank_filled = [sem(f"bank_filled{i}") for i in range(8)]
        bank_drained = [sem(f"bank_drained{i}") for i in range(8)]
        x_loaded = sem("x_loaded")
        mem_loaded = sem("mem_loaded")
        rows_loaded = sem("rows_loaded")
        small_loaded = sem("small_loaded")
        bias_loaded = sem("bias_loaded")
        gb_loaded = sem("gb_loaded")
        stored = sem("stored")
        consts_ready = sem("consts_ready")
        pool_step = sem("pool_step")
        dve_step = sem("dve_step")
        act_step = sem("act_step")
        sig_ready = sem("sig_ready")
        sig_used = sem("sig_used")
        conv_ready = sem("conv_ready")
        sq_ready = sem("sq_ready")
        stat_ready = sem("stat_ready")
        convn_ready = sem("convn_ready")
        convt_ready = sem("convt_ready")
        a_out = sem("a_out")
        gelu_in = sem("gelu_in")
        gelu_tanh = sem("gelu_tanh")
        gelu_out = sem("gelu_out")
        neg_max = sem("neg_max")
        prob_ready = sem("prob_ready")
        cmax = sem("cmax")
        cexp = sem("cexp")
        cprob = sem("cprob")
        od_c = sem("od_c")
        ln_stats = sem("ln_stats")
        ln_rstd = sem("ln_rstd")
        n_ready = sem("n_ready")
        x_ready = sem("x_ready")
        xT_half = sem("xT_half")
        gexp_in = sem("gexp_in")
        gexp = sem("gexp")
        eexp_in = sem("eexp_in")
        eexp = sem("eexp")
        mask_ready = sem("mask_ready")
        count_ready = sem("count_ready")
        passes_done = [sem(f"passes_done{L}") for L in range(DEPTH)]
        pass_over = sem("pass_over")

        class Family:

            def __init__(self, name, own_loads):
                self.w1_used = sem(f"{name}_w1_used")
                self.hid_done = sem(f"{name}_hid_done")
                self.tanh_done = sem(f"{name}_tanh_done")
                self.glu_done = sem(f"{name}_glu_done")
                self.hidden_ready = sem(f"{name}_hidden_ready")
                self.hidT_done = sem(f"{name}_hidT_done")
                self.hidT_ready = sem(f"{name}_hidT_ready")
                self.comb_done = sem(f"{name}_comb_done")
                self.comb_ready = sem(f"{name}_comb_ready")
                self.y_done = sem(f"{name}_y_done")
                self.y_ready = sem(f"{name}_y_ready")
                self.scattered = sem(f"{name}_scattered")
                self.disp_built = sem(f"{name}_disp_built")
                self.disp_gated = sem(f"{name}_disp_gated")
                self.gather_done = sem(f"{name}_gather_done")
                self.gathered = sem(f"{name}_gathered")
                self.loaded = [sem(f"{name}_loaded{i}") for i in range(RING)] if own_loads else loaded

        main = Family("first", False)
        over = [Family(f"more{L}", True) for L in range(DEPTH)]

        slot_of, slot_uses, slot_last = {}, [0] * RING, [None] * RING
        order = []
        bank_of, fills, rotation = {}, [0] * 8, [0]
        moe_base = []

        def slot(key):
            return ring[:, slot_of[key][0], :]

        def wait_loaded(eng, key):
            s, n = slot_of[key]
            eng.wait_ge(loaded[s], 16 * n)

        def claim(pe, key, bank=None):
            b = rotation[0] if bank is None else bank
            if bank is None:
                rotation[0] = (b + 1) % 8
            if fills[b]:
                pe.wait_ge(bank_drained[b], fills[b])
            fills[b] += 1
            bank_of[key] = (b, fills[b])
            return banks[b]

        def filled(ins, key):
            ins.then_inc(bank_filled[bank_of[key][0]], 1)

        def wait_filled(eng, key):
            b, n = bank_of[key]
            eng.wait_ge(bank_filled[b], n)
            return banks[b]

        def drained(ins, key):
            ins.then_inc(bank_drained[bank_of[key][0]], 1)

        def wait_drained(eng, key):
            b, n = bank_of[key]
            eng.wait_ge(bank_drained[b], n)

        block = ctx.enter_context(nc.Block())

        @block.sync
        def _(sp):
            at = [0]

            def load(key, dst_view, src):
                s = at[0] % RING
                at[0] += 1
                last = slot_last[s]
                if last is not None:
                    sp.wait_ge(last[0], last[1])
                slot_uses[s] += 1
                slot_of[key] = (s, slot_uses[s])
                order.append(key)
                slot_last[s] = (weights_used, len(order))
                sp.dma_start(dst_view(ring[:, s, :]), src).then_inc(loaded[s], 16)

            def load_cols(key, w, c0, n=512):
                load(key, lambda r: r[:, 0:KC * n].rearrange("p (k n) -> p k n", k=KC),
                     w[:, c0:c0 + n].rearrange("(p k) n -> p k n", k=KC))

            def load_out(key, w, c0):
                load(key, lambda r: r.rearrange("p (k n) -> p k n", k=KC),
                     w[:, c0:c0 + 512].rearrange("(k p) n -> p k n", p=P))

            sp.dma_start(x[:, :, :], T["x"][0].rearrange("(t p) d -> p t d", p=P)).then_inc(x_loaded, 16)
            load_cols("av", T["ev_w_in"][0], 0)
            load_cols("ag", T["ev_w_in"][0], 512)
            sp.dma_start(rows1[0:TAPS * CC, :], T["ev_conv_w"][0].rearrange("j (c p) -> (j c) p", p=P)).then_inc(rows_loaded, 16)
            for c, n in ((C_CB, "ev_conv_b"), (C_CG, "ev_cnorm_g"), (C_CN, "ev_cnorm_b")):
                sp.dma_start(rows2[c:c + CC, :], T[n][0].rearrange("(c p) -> c p", p=P)).then_inc(rows_loaded, 16)
            sp.dma_start(rows2[C_OD:C_OD + 24, :], T["od_conv_w"][0].rearrange("j (c p) -> (j c) p", p=P)).then_inc(rows_loaded, 16)
            for c, n in ((C_PK, "ev_cmp_pe_k"), (C_PV, "ev_cmp_pe_v")):
                sp.dma_start(rows2[c:c + 16, :], T[n][0].rearrange("(j l) d -> j (l d)", l=2)).then_inc(rows_loaded, 16)
            sp.dma_start(gb[:, :, :], T["mem"][0].rearrange("(t p) d -> p t d", p=P)).then_inc(mem_loaded, 16)
            load_cols("q", T["ev_w_in"][0], 1024)
            load_cols("kv", T["ev_w_in"][0], 1536)
            load_cols("kw", T["ev_w_in"][0], 2048, 280)
            load_cols("mk0", T["mem_wk"], 0)
            load_cols("mk1", T["mem_wk"], 512)
            for b, n in enumerate(("ev_cmp_w1_k", "ev_cmp_w1_v")):
                load(f"c{b}", lambda r: r.rearrange("p (j n) -> p j n", j=16),
                     T[n][0].rearrange("(j p) n -> p j n", p=P))
            load_cols("mv0", T["mem_wv"], 0)
            load_cols("mv1", T["mem_wv"], 512)

            def load_experts(L, q, i, fam, sems, first):
                for j in range(2):
                    for m, name in enumerate(("moe_w1", "moe_w3", "moe_w2")):
                        s = 3 * j + m
                        if not first:
                            sp.wait_ge((fam.w1_used, fam.hid_done, fam.y_done)[m], q * NE + i * 2 + (j - 1))
                        w = T[name][L].rearrange("(i j) a b -> i j a b", j=2)[i, j]
                        if m < 2:
                            sp.dma_start(ring[:, s, :].rearrange("p (k n) -> p k n", k=KC),
                                         w.rearrange("(p k) n -> p k n", k=KC)).then_inc(sems[s], 16)
                        else:
                            sp.dma_start(ring[:, s, :].rearrange("p (h c n) -> p h c n", h=2, c=2),
                                         w.rearrange("(h p c) n -> p h c n", h=2, c=2)).then_inc(sems[s], 16)

            for L in range(DEPTH):
                if L == 0:
                    load_out("wo_mix0a", T["ev_w_out"][0], 0)
                    load_out("wo_mix0b", T["ev_w_out"][0], 512)
                else:
                    for h in range(2):
                        for part, c0 in (("c", D), ("h", 2 * D), ("b", 0)):
                            load_cols(f"od_{part}{h}", T["od_w_in"][0], c0 + 512 * h)
                    load_out("wo_mix1a", T["od_w_out"][0], 0)
                    load_out("wo_mix1b", T["od_w_out"][0], 512)
                for h in range(2):
                    load_cols(f"xq{L}{h}", T["xa_wq"][L], 512 * h)
                for h in range(2):
                    load_out(f"xo{L}{'ab'[h]}", T["xa_wo"][L], 512 * h)
                for s in range(RING):
                    if slot_last[s] is not None:
                        sp.wait_ge(slot_last[s][0], slot_last[s][1])
                    j, m = divmod(s, 3)
                    w = T[("moe_w1", "moe_w3", "moe_w2")[m]][L, j]
                    if m < 2:
                        sp.dma_start(ring[:, s, :].rearrange("p (k n) -> p k n", k=KC),
                                     w.rearrange("(p k) n -> p k n", k=KC)).then_inc(loaded[s], 16)
                    else:
                        sp.dma_start(ring[:, s, :].rearrange("p (h c n) -> p h c n", h=2, c=2),
                                     w.rearrange("(h p c) n -> p h c n", h=2, c=2)).then_inc(loaded[s], 16)
                moe_base.append(list(slot_uses))
                with sp.Fori(1, PAIRS) as i:
                    load_experts(L, L, i, main, loaded, False)
                for s in range(RING):
                    j, m = divmod(s, 3)
                    slot_uses[s] += PAIRS
                    slot_last[s] = ((main.w1_used, main.hid_done, main.y_done)[m], (L + 1) * NE - 1 + j)
                at[0] = 0
                sp.wait_ge(count_ready, L + 1)
                longest = sp.value_load(mosti[0:1, 0:1], min_val=0, max_val=S)
                with sp.Fori(0, PASSES - 1) as q:
                    with sp.If(longest > q * CAP + CAP):
                        sp.wait_ge(passes_done[L], q + 1)
                        load_experts(L, q, 0, over[L], over[L].loaded, True)
                        with sp.Fori(1, PAIRS) as i:
                            load_experts(L, q, i, over[L], over[L].loaded, False)
                        sp.wait_ge(over[L].y_done, q * NE + NE)
                        sp.sem_inc(pass_over, 1)
            sp.wait_ge(x_ready, 2 * LN_COUNT)
            sp.dma_start(out[0].rearrange("(t p) d -> p t d", p=P), x[:, :, :]).then_inc(stored, 16)
            sp.wait_ge(stored, 16)

        @block.tensor
        def _(pe):
            mm = nc.tensor.matmul
            used = [0]

            def release(ins, key):
                assert order[used[0]] == key, (order[used[0]], key)
                used[0] += 1
                ins.then_inc(weights_used, 1)

            def transposed(key, src):
                for t in range(TT):
                    if key[0] == "n":
                        pe.wait_ge(n_ready, 2 * key[1] + t + 1)
                    for h in range(2):
                        ps = claim(pe, (key, t, h))
                        for k in range(4):
                            cols_ = src[:, t, :].rearrange("p (q k) -> p k q", k=KC)[:, 4 * h + k, :]
                            ins = nc.tensor.transpose(ps[:, k * P:(k + 1) * P], cols_, ident[:, :])
                        filled(ins, (key, t, h))

            def wait_xT(key):
                for t in range(TT):
                    for h in range(2):
                        wait_drained(pe, (key, t, h))

            def by_weight(key, wkey, c0, rhs, ps, last):
                w = slot(wkey)[:, 0:KC * last].rearrange("p (k n) -> p k n", k=KC)
                for k in range(KC):
                    ins = mm(ps, w[:, k, c0:c0 + P], rhs[:, k, :], start=(k == 0), stop=(k == KC - 1))
                return ins

            def out_projection(name, i):
                for h in range(2):
                    wkey = f"{name}{'ab'[h]}"
                    wait_loaded(pe, wkey)
                    w = slot(wkey).rearrange("p (k n) -> p k n", k=KC)
                    for t in range(TT):
                        ps = claim(pe, ("f", i, t, h))
                        for k in range(KC):
                            ins = mm(ps[:, :], oT[:, k, t * P:(t + 1) * P], w[:, k, :], start=(k == 0), stop=(k == KC - 1))
                        filled(ins, ("f", i, t, h))
                    pe.wait_ge(bank_filled[bank_of[("f", i, TT - 1, h)][0]], bank_of[("f", i, TT - 1, h)][1])
                    release(pe.nop(), wkey)

            def signal_release(key, tile):
                b, n = bank_of[tile]
                pe.wait_ge(bank_filled[b], n)
                release(pe.nop(), key)

            pe.wait_ge(consts_ready, 1)
            pe.wait_ge(x_loaded, 16)
            transposed(("x",), x)
            pe.wait_ge(rows_loaded, 16 * 7)
            ps = claim(pe, ("cols",))
            nc.tensor.transpose(ps[:, 0:TAPS * CC], rows1[0:TAPS * CC, :], ident[0:TAPS * CC, 0:TAPS * CC])
            filled(nc.tensor.transpose(ps[:, 128:128 + C_ALL], rows2[0:C_ALL, :], ident[0:C_ALL, 0:C_ALL]), ("cols",))

            wait_xT(("x",))
            wait_loaded(pe, "av")
            wait_loaded(pe, "ag")
            for c in range(CC):
                ps = claim(pe, ("a", c))
                by_weight(None, "av", c * P, xT, ps[:, 0:S], 512)
                ins = by_weight(None, "ag", c * P, xT, ps[:, S:2 * S], 512)
                filled(ins, ("a", c))
            signal_release("av", ("a", CC - 1))
            release(pe.nop(), "ag")
            pe.wait_ge(mem_loaded, 16)
            transposed(("mem",), gb)

            wait_loaded(pe, "q")
            for j in range(2):
                ps = claim(pe, ("q", j))
                for c in range(2):
                    ins = by_weight(None, "q", (2 * j + c) * P, xT, ps[:, c * S:(c + 1) * S], 512)
                filled(ins, ("q", j))
            signal_release("q", ("q", 1))
            wait_loaded(pe, "kv")
            wait_loaded(pe, "kw")
            wkv = slot("kv").rearrange("p (k n) -> p k n", k=KC)
            wkw = slot("kw")[:, 0:KC * 280].rearrange("p (k n) -> p k n", k=KC)
            for b in range(2):
                ps = claim(pe, ("z", b))
                for g in range(2):
                    c0 = b * P + g * HD
                    for k in range(KC):
                        mm(ps[0:HD, g * S:(g + 1) * S], wkv[:, k, c0:c0 + HD], xT[:, k, :], start=(k == 0), stop=(k == KC - 1))
                        ins = mm(ps[HD:P, g * S:(g + 1) * S - 1], wkv[:, k, c0:c0 + HD], xT[:, k, 1:S], start=(k == 0), stop=(k == KC - 1))
                filled(ins, ("z", b))
            for g in range(2):
                ps = claim(pe, ("k", g))
                for b, (w, c0) in enumerate(((wkv, 2 * P), (wkw, 0))):
                    for k in range(KC):
                        for r in range(2):
                            ins = mm(ps[r * HD:(r + 1) * HD, b * S:(b + 1) * S], w[:, k, c0 + g * HD:c0 + (g + 1) * HD],
                                     xT[:, k, :], start=(k == 0), stop=(k == KC - 1))
                filled(ins, ("k", g))
            for t in range(TT):
                ps = claim(pe, ("v", t))
                for k in range(KC):
                    mm(ps[:, 0:P], xT[:, k, t * P:(t + 1) * P], wkv[:, k, 3 * P:4 * P], start=(k == 0), stop=(k == KC - 1))
                for k in range(KC):
                    ins = mm(ps[:, P:P + 152], xT[:, k, t * P:(t + 1) * P], wkw[:, k, P:280], start=(k == 0), stop=(k == KC - 1))
                filled(ins, ("v", t))
            signal_release("kv", ("v", TT - 1))
            release(pe.nop(), "kw")

            wait_xT(("mem",))
            for j in range(4):
                wkey = f"mk{j // 2}"
                if j % 2 == 0:
                    wait_loaded(pe, wkey)
                ps = claim(pe, ("mk", j))
                for c in range(2):
                    ins = by_weight(None, wkey, ((2 * j + c) % 4) * P, memT, ps[:, c * S:(c + 1) * S], 512)
                filled(ins, ("mk", j))
                if j % 2:
                    signal_release(wkey, ("mk", j))

            for b in range(2):
                wait_drained(pe, ("z", b))
            ps = claim(pe, ("ch",))
            for b in range(2):
                wait_loaded(pe, f"c{b}")
                w = slot(f"c{b}").rearrange("p (j n) -> p j n", j=16)
                for h in range(2):
                    o = (2 * b + h) * 32
                    for j in range(16):
                        ins = mm(ps[:, o:o + 2 * NCMP], w[:, j, h * P:(h + 1) * P],
                                 blocks[:, b, j, :, :].rearrange("p g n -> p (g n)"), start=(j == 0), stop=(j == 15))
            filled(ins, ("ch",))
            signal_release("c0", ("ch",))
            release(pe.nop(), "c1")

            for h in range(2):
                wkey = f"mv{h}"
                wait_loaded(pe, wkey)
                w = slot(wkey).rearrange("p (k n) -> p k n", k=KC)
                for t in range(TT):
                    ps = claim(pe, ("mv", t, h))
                    for k in range(KC):
                        ins = mm(ps[:, :], memT[:, k, t * P:(t + 1) * P], w[:, k, :], start=(k == 0), stop=(k == KC - 1))
                    filled(ins, ("mv", t, h))
                signal_release(wkey, ("mv", TT - 1, h))

            pe.wait_ge(gelu_out, 1)
            pe.wait_ge(small_loaded, 16 * 12)
            ps = claim(pe, ("c2",))
            for g in range(2):
                for h in range(2):
                    for r in range(2):
                        mm(ps[r * HD:(r + 1) * HD, g * 16:g * 16 + NCMP], w2c[:, 0, h, :],
                           ghid[:, h, g * NCMP:(g + 1) * NCMP], start=(h == 0), stop=(h == 1))
            for g in range(2):
                for h in range(2):
                    ins = mm(ps[0:NCMP, 64 + g * HD:64 + (g + 1) * HD], ghid[:, 2 + h, g * NCMP:(g + 1) * NCMP],
                             w2c[:, 1, h, :], start=(h == 0), stop=(h == 1))
            filled(ins, ("c2",))

            pe.wait_ge(consts_ready, 2)
            ps = claim(pe, ("cmean",))
            for c in range(CC):
                pe.wait_ge(conv_ready, c + 1)
                ins = mm(ps[:, 0:S], onesc[:, :], oT[:, c, :], start=(c == 0), stop=(c == CC - 1))
            filled(ins, ("cmean",))

            for j in range(2):
                wait_drained(pe, ("q", j))
            wait_drained(pe, ("c2",))
            for r in range(2):
                ps = claim(pe, ("sc", r))
                rr = slice(r * HD, (r + 1) * HD)
                for t in range(TT):
                    for c in range(CC):
                        ins = mm(ps[:, (t * CC + c) * 16:(t * CC + c) * 16 + NCMP], qT[rr, c, t * P:(t + 1) * P],
                                 k_cmpT[rr, c // 2, 0:NCMP], start=True, stop=True)
                filled(ins, ("sc", r))
            for g in range(2):
                wait_drained(pe, ("k", g))

            def scores(h):
                c, r = h // 2, h % 2
                rr = slice(r * HD, (r + 1) * HD)
                kk = kT[rr, c // 2, :].rearrange("p (b k) -> p b k", b=2)
                for t in range(TT):
                    n = (t + 1) * P
                    ps = claim(pe, ("s", h, t))
                    ins = mm(ps[:, 0:2 * n], qT[rr, c, t * P:(t + 1) * P], kk[:, :, 0:n], start=True, stop=True)
                    filled(ins, ("s", h, t))

            def attend(h):
                c, r = h // 2, h % 2
                g = c // 2
                pT = claim(pe, ("pT", h, 0))
                pU = claim(pe, ("pT", h, 1))
                pe.wait_ge(prob_ready, 2 * h + 1)
                for b in range(2):
                    nc.tensor.transpose(pT[:, b * P:(b + 1) * P], prob[:, h % 2, 0, b * P:(b + 1) * P], ident[:, :])
                for t in range(TT):
                    ins = nc.tensor.transpose(pT[0:16, (2 + t) * P:(3 + t) * P], pc[:, t, h, :], ident[:, :])
                filled(ins, ("pT", h, 0))
                pe.wait_ge(prob_ready, 2 * h + 2)
                for b in range(2):
                    for kt in range(2):
                        ins = nc.tensor.transpose(pU[:, (2 * b + kt) * P:(2 * b + kt + 1) * P],
                                                  prob[:, h % 2, 1, b * S + kt * P:b * S + (kt + 1) * P], ident[:, :])
                filled(ins, ("pT", h, 1))

            def weigh(h):
                c, r = h // 2, h % 2
                g = c // 2
                ps = claim(pe, ("o", c)) if r == 0 else banks[bank_of[("o", c)][0]]
                po = ps[r * HD:(r + 1) * HD, 0:S]
                wait_drained(pe, ("pT", h, 0))
                wait_drained(pe, ("pT", h, 1))
                for b in range(2):
                    mm(po, v_sb[:, 0, b, g * HD:(g + 1) * HD], probT[:, h % 2, b, 0, :], start=(b == 0), stop=False)
                    mm(po[:, P:S], v_sb[:, 1, b, g * HD:(g + 1) * HD], probT[:, h % 2, b, 1, P:S], start=False, stop=False)
                ins = mm(po, v_cmp[0:NCMP, g, :], pcT[0:NCMP, h % 2, :], start=False, stop=True)
                if r == 1:
                    filled(ins, ("o", c))

            pe.wait_ge(cprob, 1)
            for t in range(TT):
                wait_drained(pe, ("v", t))
            scores(0)
            for h in range(HEADS):
                if h + 1 < HEADS:
                    scores(h + 1)
                attend(h)
                if h > 0:
                    weigh(h - 1)
                if h == 2:
                    ps = claim(pe, ("cvar",))
                    for c in range(CC):
                        pe.wait_ge(sq_ready, c + 1)
                        ins = mm(ps[:, 0:S], onesc[:, :], aT[:, c, PAD:PAD + S], start=(c == 0), stop=(c == CC - 1))
                    filled(ins, ("cvar",))
            weigh(HEADS - 1)
            pe.wait_ge(a_out, CC)
            for c in range(CC):
                wait_drained(pe, ("o", c))

            for L in range(DEPTH):
                if L == 1:
                    wait_xT(("n", 2))
                    for h in range(2):
                        for part in "chb":
                            wait_loaded(pe, f"od_{part}{h}")
                        for c in range(4):
                            ps = claim(pe, ("odc", 4 * h + c))
                            by_weight(None, f"od_c{h}", c * P, xT, ps[:, 0:S], 512)
                            filled(by_weight(None, f"od_h{h}", c * P, xT, ps[:, S:2 * S], 512), ("odc", 4 * h + c))
                            ps = claim(pe, ("odb", 4 * h + c))
                            filled(by_weight(None, f"od_b{h}", c * P, xT, ps[:, 0:S], 512), ("odb", 4 * h + c))
                        signal_release(f"od_c{h}", ("odb", 4 * h + 3))
                        release(pe.nop(), f"od_h{h}")
                        release(pe.nop(), f"od_b{h}")
                    for c in range(KC):
                        wait_drained(pe, ("odb", c))
                out_projection(f"wo_mix{L}", 3 * L)

                transposed(("n", 3 * L), x)
                wait_xT(("n", 3 * L))
                for j in range(4):
                    wkey = f"xq{L}{j // 2}"
                    if j % 2 == 0:
                        wait_loaded(pe, wkey)
                    ps = claim(pe, ("xq", L, j))
                    for c in range(2):
                        ins = by_weight(None, wkey, ((2 * j + c) % 4) * P, xT, ps[:, c * S:(c + 1) * S], 512)
                    filled(ins, ("xq", L, j))
                    if j % 2:
                        signal_release(wkey, ("xq", L, j))
                if L == 0:
                    for j in range(4):
                        wait_drained(pe, ("mk", j))
                        wait_drained(pe, ("mv", j % 2, j // 2))

                def xscores(h):
                    wait_drained(pe, ("xq", L, h))
                    ps = claim(pe, ("xs", L, h))
                    for t in range(TT):
                        for c in range(2):
                            ins = mm(ps[:, t * S:(t + 1) * S], qxT[:, 2 * h + c, t * P:(t + 1) * P],
                                     mem_kT[:, 2 * h + c, :], start=(c == 0), stop=(c == 1))
                    filled(ins, ("xs", L, h))

                def xattend(h):
                    pe.wait_ge(prob_ready, 2 * HEADS + L * XH + h + 1)
                    ps = claim(pe, ("xp", L, h))
                    for m in range(2):
                        for t in range(TT):
                            ins = nc.tensor.transpose(ps[:, (2 * m + t) * P:(2 * m + t + 1) * P],
                                                      prob[:, h % 2, t, m * P:(m + 1) * P], ident[:, :])
                    filled(ins, ("xp", L, h))

                def xweigh(h):
                    wait_drained(pe, ("xp", L, h))
                    ps = claim(pe, ("xo", L, h))
                    for c in range(2):
                        for m in range(2):
                            ins = mm(ps[:, c * S:(c + 1) * S], mem_v[:, m, (2 * h + c) * P:(2 * h + c + 1) * P],
                                     probT[:, h % 2, 0, m, :], start=(m == 0), stop=(m == 1))
                    filled(ins, ("xo", L, h))

                xscores(0)
                for h in range(XH):
                    if h + 1 < XH:
                        xscores(h + 1)
                    xattend(h)
                    if h > 0:
                        xweigh(h - 1)
                xweigh(XH - 1)
                for h in range(XH):
                    wait_drained(pe, ("xo", L, h))
                out_projection(f"xo{L}", 3 * L + 1)

                transposed(("n", 3 * L + 1), x)
                wait_xT(("n", 3 * L + 1))
                ps = claim(pe, ("lg", L))
                for t in range(TT):
                    for k in range(KC):
                        ins = mm(ps[:, t * 64:t * 64 + NG + NE], xT[:, k, t * P:(t + 1) * P], wr[:, L, k, :],
                                 start=(k == 0), stop=(k == KC - 1))
                filled(ins, ("lg", L))
                pe.wait_ge(mask_ready, L + 1)
                ps = claim(pe, ("pos", L))
                mm(ps[:, 0:NE], tri[:, :], mask[:, 0, :], start=True, stop=True)
                mm(ps[:, NE:2 * NE], tri[:, :], mask[:, 1, :], start=True, stop=False)
                mm(ps[:, NE:2 * NE], ones[:, :], mask[:, 0, :], start=False, stop=True)
                mm(ps[:, 64:64 + NE], ones[:, :], mask[:, 0, :], start=True, stop=False)
                filled(mm(ps[:, 64:64 + NE], ones[:, :], mask[:, 1, :], start=False, stop=True), ("pos", L))

                acc = []
                for t in range(TT):
                    for h in range(2):
                        acc.append(claim(pe, ("f", 3 * L + 2, t, h), bank=2 * t + h))
                for b in range(4, 8):
                    pe.wait_ge(bank_drained[b], fills[b])
                rotation[0] = 4
                bH, bY, bT, bG = banks[4:8]
                for a in acc:
                    mm(a[:, :], zero16[:, 0:P], zero16[:, :], start=True, stop=False, skip_group_check=True)

                def gather(fam, n, h, clear=False):
                    if not clear:
                        pe.wait_ge(fam.gathered, n * 2 + h)
                    for k in range(4):
                        for t in range(TT):
                            src = x[:, t, :].rearrange("p (q k) -> p k q", k=KC)[:, 4 * h + k, :]
                            ins = mm(bG[:, k * P:(k + 1) * P], src, disp[:, t, :, :].rearrange("p e s -> p (e s)"),
                                     start=(t == 0), stop=(t == TT - 1))
                    ins.then_inc(fam.gather_done, 1)

                def scatter(fam, b):
                    for t in range(TT):
                        for h in range(2):
                            hh = slice(h * CAP, (h + 1) * CAP)
                            ins = mm(acc[2 * t + h][:, :], comb[hh, b, t * P:(t + 1) * P], y[hh, b, :],
                                     start=False, stop=False, skip_group_check=True)
                    ins.then_inc(fam.scattered, 1)

                def expert_pass(fam, q, sems, base):
                    pe.wait_ge(fam.disp_built, q * 17 + 1)
                    gather(fam, q * 17, 0, clear=True)
                    gather(fam, q * 17, 1)
                    with pe.Fori(0, PAIRS) as i:
                        for j in range(2):
                            e1 = q * NE + i * 2 + (j + 1)
                            w1, w3 = (ring[:, 3 * j + m, :].rearrange("p (k n) -> p k n", k=KC) for m in range(2))
                            w2 = ring[:, 3 * j + 2, :].rearrange("p (h c n) -> p h c n", h=2, c=2)
                            if j == 0:
                                pe.wait_ge(fam.gathered, (q * 17 + i) * 2 + 2)
                            for m, w in enumerate((w1, w3)):
                                pe.wait_ge(sems[3 * j + m], (i + (base(3 * j + m) + 1)) * 16)
                                for k in range(KC):
                                    for n in range(2):
                                        ins = mm(bH[n * CAP:(n + 1) * CAP, m * S:(m + 1) * S], xgT[:, k, j * CAP:(j + 1) * CAP],
                                                 w[:, k, n * S:(n + 1) * S], start=(k == 0), stop=(k == KC - 1), skip_group_check=True)
                                ins.then_inc((fam.w1_used, fam.hid_done)[m], 1)
                            if j == 1:
                                pe.wait_ge(fam.disp_built, q * 17 + i + 2)
                                gather(fam, q * 17 + i + 1, 0)
                            pe.wait_ge(fam.y_ready, q * 33 + i * 2 + (j + 1))
                            pe.wait_ge(fam.comb_ready, q * 33 + i * 2 + (j + 1))
                            scatter(fam, 1 - j)
                            pe.wait_ge(fam.disp_gated, q * 17 + i + 1)
                            for t in range(TT):
                                ins = nc.tensor.transpose(bY[:, t * P:(t + 1) * P],
                                                          dispg[:, j, t, :, :].rearrange("p a s -> p (a s)"), ident[:, :])
                            ins.then_inc(fam.comb_done, 1)
                            if j == 1:
                                gather(fam, q * 17 + i + 1, 1)
                            pe.wait_ge(fam.hidden_ready, e1)
                            for c in range(2):
                                ins = nc.tensor.transpose(bT[:, c * P:(c + 1) * P],
                                                          hid[:, :].rearrange("p (q c) -> p c q", c=2)[:, c, :], ident[:, :])
                            ins.then_inc(fam.hidT_done, 1)
                            pe.wait_ge(sems[3 * j + 2], (i + (base(3 * j + 2) + 1)) * 16)
                            pe.wait_ge(fam.hidT_ready, e1)
                            pe.wait_ge(fam.comb_ready, q * 33 + i * 2 + (j + 2))
                            for h in range(2):
                                for c in range(2):
                                    for n in range(2):
                                        ins = mm(bY[n * CAP:(n + 1) * CAP, :], hidT[:, c, h * CAP:(h + 1) * CAP],
                                                 w2[:, h, c, n * 512:(n + 1) * 512], start=(h + c == 0), stop=(h + c == 2),
                                                 skip_group_check=True)
                            ins.then_inc(fam.y_done, 1)
                    pe.wait_ge(fam.y_ready, q * 33 + 33)
                    pe.wait_ge(fam.comb_ready, q * 33 + 33)
                    scatter(fam, 1)
                    pe.wait_ge(fam.gathered, (q * 17 + 17) * 2)
                    pe.wait_ge(fam.scattered, q * 33 + 33)
                    pe.sem_inc(passes_done[L], 1)

                for t in range(TT):
                    pe.wait_ge(x_ready, 2 * (3 * L + 1) + t + 1)
                expert_pass(main, L, loaded, lambda s: moe_base[L][s])
                pe.wait_ge(count_ready, L + 1)
                longest = pe.value_load(mosti[0:1, 0:1], min_val=0, max_val=S)
                with pe.Fori(0, PASSES - 1) as q:
                    with pe.If(longest > q * CAP + CAP):
                        expert_pass(over[L], q, over[L].loaded, lambda s: q * PAIRS)
                for t in range(TT):
                    for h in range(2):
                        key = ("f", 3 * L + 2, t, h)
                        filled(mm(acc[2 * t + h][:, :], zero16[:, 0:P], zero16[:, :], start=False, stop=True,
                                  skip_group_check=True), key)
                if L + 1 < DEPTH:
                    transposed(("n", 3 * L + 2), x)

        def norm_dve(st, v, i):
            for t in range(TT):
                for h in range(2):
                    key = ("f", i, t, h)
                    ps = wait_filled(v, key)
                    xx = x[:, t, h * 512:(h + 1) * 512]
                    drained(nc.vector.scalar_tensor_tensor(out=xx, in0=xx, scalar=ALPHA, in1=ps[:, :], op0=ALU.mult, op1=ALU.add), key)
                for h in range(2):
                    wait_drained(v, ("f", i, t, h))
                    st.mark(nc.vector.bn_stats(out=bn[:, t, h, :], in_=x[:, t, h * 512:(h + 1) * 512]))
                st.wait()
                nc.vector.bn_aggr(out=mv[:, t, :], in_=bn[:, t, :, :].rearrange("p a b -> p (a b)")).then_inc(ln_stats, 1)
            for t in range(TT):
                v.wait_ge(ln_rstd, 2 * i + t + 1)
                nc.vector.tensor_scalar(x[:, t, :], x[:, t, :], mv[:, t, 0:1], rstd[:, t, :], ALU.subtract, ALU.mult).then_inc(n_ready, 1)
            if i == 0:
                v.wait_ge(small_loaded, 16 * 12)
            if i < LN_COUNT - 1:
                for t in range(TT):
                    ps = wait_filled(v, (("n", i), t, 1))
                    pv = ps[:, :].rearrange("p (k s) -> p k s", k=4)
                    o = xT[:, 4:8, t * P:(t + 1) * P]
                    st.do(nc.vector.tensor_tensor(o, pv, lngT[:, i, 0, 4:8].unsqueeze(2).to_broadcast([P, 4, P]), ALU.mult))
                    drained(nc.vector.tensor_tensor(o, o, lngT[:, i, 1, 4:8].unsqueeze(2).to_broadcast([P, 4, P]), ALU.add), (("n", i), t, 1))
            v.wait_ge(gb_loaded, 32 * (i + 1))
            for t in range(TT):
                if i < LN_COUNT - 1:
                    wait_filled(v, (("n", i), t, 0))
                else:
                    v.wait_ge(n_ready, 2 * i + t + 1)
                st.mark(nc.vector.tensor_tensor(x[:, t, :], x[:, t, :], gb[:, 0, :], ALU.mult))
            a = st.n
            for t in range(TT):
                st.wait(a - 1 + t)
                nc.vector.tensor_tensor(x[:, t, :], x[:, t, :], gb[:, 1, :], ALU.add).then_inc(x_ready, 1)

        def norm_act(a, i):
            for t in range(TT):
                ps = wait_filled(a, (("n", i), t, 0))
                for k in range(4):
                    ins = nc.scalar.activation(xT[:, k, t * P:(t + 1) * P], ps[:, k * P:(k + 1) * P], ACT.Identity,
                                               scale=lngT[:, i, 0, k:k + 1], bias=lngT[:, i, 1, k:k + 1])
                drained(ins, (("n", i), t, 0))

        @block.vector
        def _(v):
            st = Steps(v, dve_step)
            tt, ts, stt, cp = nc.vector.tensor_tensor, nc.vector.tensor_scalar, nc.vector.scalar_tensor_tensor, nc.vector.tensor_copy

            nc.vector.memset(aT[:, :, 0:PAD], 0.0)
            nc.vector.memset(g8[:, :, :], NEG)
            nc.vector.memset(place[:, :, NE:NE + 2], -1.0)
            nc.vector.memset(gate[:, :, NE:NE + 2], 0.0)
            st.do(nc.vector.memset(pc[:, :, :, :], 0.0))
            zeros_set = st.n
            for t in range(TT):
                for h in range(2):
                    if h:
                        ps = wait_filled(v, (("x",), t, h))
                        drained(cp(xT[:, 4 * h:4 * h + 4, t * P:(t + 1) * P], ps[:, :].rearrange("p (k s) -> p k s", k=4)), (("x",), t, h))
            ps = wait_filled(v, ("cols",))
            ts(cw[:, 0:TAPS * CC], ps[:, 0:TAPS * CC], 0.5, None, ALU.mult)
            drained(cp(cols[:, :], ps[:, P:P + C_ALL]), ("cols",))
            wait_drained(v, ("cols",))
            for c in range(CC):
                v.wait_ge(sig_ready, c + 1)
                ps = banks[bank_of[("a", c)][0]]
                drained(stt(out=aT[:, c, PAD:PAD + S], in0=scr[:, c % 2, :], scalar=1.0, in1=ps[:, 0:S], op0=ALU.add, op1=ALU.mult), ("a", c))
            for t in range(TT):
                ps = wait_filled(v, (("mem",), t, 1))
                drained(cp(memT[:, 4:8, t * P:(t + 1) * P], ps[:, :].rearrange("p (k s) -> p k s", k=4)), (("mem",), t, 1))
            for c in range(CC):
                wait_drained(v, ("a", c))
            def compress_input(b):
                ps = wait_filled(v, ("z", b))
                tok = ps[:, :].rearrange("p (g a r two) -> p r g a two", g=2, a=16, two=2)[:, :, :, :, 0]
                for jh in range(2):
                    pe_ = cols[:, (C_PK, C_PV)[b] + 8 * jh:(C_PK, C_PV)[b] + 8 * jh + 8]
                    for g in range(2):
                        ins = tt(blocks[:, b, 8 * jh:8 * jh + 8, g, :], tok[:, :, g, jh:jh + NCMP],
                                 pe_.unsqueeze(2).to_broadcast([P, 8, NCMP]), ALU.add)
                drained(ins, ("z", b))

            base = st.n
            for k in range(TAPS):
                for c in range(CC):
                    w = cw[:, k * CC + c:k * CC + c + 1]
                    src = aT[:, c, k:k + S]
                    if k == 0:
                        st.mark(ts(oT[:, c, :], src, w, cols[:, C_CB + c:C_CB + c + 1], ALU.mult, ALU.add))
                        continue
                    st.wait(base + (k - 1) * CC + c + 1)
                    ins = stt(out=oT[:, c, :], in0=src, scalar=w, in1=oT[:, c, :], op0=ALU.mult, op1=ALU.add)
                    if k < TAPS - 1:
                        st.mark(ins)
                    else:
                        ins.then_inc(conv_ready, 1)
            compress_input(0)
            compress_input(1)
            ps = wait_filled(v, ("ch",))
            hv = ps[:, 0:P].rearrange("p (a n) -> p a n", n=32)[:, :, 0:2 * NCMP]
            hh, gt = ghid[:, :, 0:2 * NCMP], gtmp[:, :, 0:2 * NCMP]
            st.do(cp(hh, hv))
            st.do(tt(gt, hh, hh, ALU.mult))
            st.do(ts(gt, gt, GELU_A, 1.0, ALU.mult, ALU.add))
            drained(tt(gt, gt, hh, ALU.mult), ("ch",))
            v.wait_ge(gelu_tanh, 1)
            stt(out=hh, in0=gt, scalar=1.0, in1=hh, op0=ALU.add, op1=ALU.mult).then_inc(gelu_out, 1)
            wait_drained(v, ("v", 0))
            wait_drained(v, ("v", 1))
            st.do(ts(gates[:, :, :], gates[:, :, :], 0.5, 0.5, ALU.mult, ALU.add))

            ps = wait_filled(v, ("cmean",))
            for c in range(CC):
                ins = tt(oT[:, c, :], oT[:, c, :], ps[:, 0:S], ALU.subtract)
                if c < CC - 1:
                    st.mark(ins)
            drained(ins, ("cmean",))
            wait_drained(v, ("cmean",))
            for c in range(CC):
                tt(aT[:, c, PAD:PAD + S], oT[:, c, :], oT[:, c, :], ALU.mult).then_inc(sq_ready, 1)

            st.wait(zeros_set)
            v.wait_ge(consts_ready, 2)
            gv = gates[:, :, :].rearrange("p t (h b) -> p t h b", b=3)
            for r in range(2):
                ps = wait_filled(v, ("sc", r))
                for t in range(TT):
                    sv = ps[:, t * 64:(t + 1) * 64].rearrange("p (c n) -> p c n", n=16)[:, :, 0:NCMP]
                    pv = pc[:, t, :, :].rearrange("p (c r) n -> p r c n", r=2)[:, r, :, 0:NCMP]
                    ins = tt(pv, sv, cbias[:, t, 0:NCMP].unsqueeze(1).to_broadcast([P, CC, NCMP]), ALU.add)
                    if t == 0:
                        st.mark(ins)
                drained(ins, ("sc", r))
                wait_drained(v, ("sc", r))
            pcv = pc[:, :, :, 0:NCMP]
            mx = stat[:, 0:16].rearrange("p (t h) -> p t h", t=TT)
            sm = stat[:, 16:32].rearrange("p (t h) -> p t h", t=TT)
            st.do(nc.vector.tensor_reduce(mx, pcv, AX, ALU.max))
            for t in range(TT):
                ins = tt(pc[:, t, :, 0:NCMP], pc[:, t, :, 0:NCMP], mx[:, t, :].unsqueeze(2).to_broadcast([P, HEADS, NCMP]), ALU.subtract)
                if t == 0:
                    st.mark(ins)
            ins.then_inc(cmax, 1)
            v.wait_ge(cexp, 1)
            st.do(nc.vector.tensor_reduce(sm, pcv, AX, ALU.add))
            st.do(nc.vector.reciprocal(sm, sm))
            st.do(tt(sm, sm, gv[:, :, :, 0], ALU.mult))
            for t in range(TT):
                w = pc[:, t, :, 0:NCMP]
                st.do(tt(w, w, sm[:, t, :].unsqueeze(2).to_broadcast([P, HEADS, NCMP]), ALU.mult))
                ins = tt(w, w, cmask[:, t, 0:NCMP].unsqueeze(1).to_broadcast([P, HEADS, NCMP]), ALU.mult)
                if t == 0:
                    st.mark(ins)
            ins.then_inc(cprob, 1)

            def soft_in(h, t):
                n = (t + 1) * P
                ps = wait_filled(v, ("s", h, t))
                sv = ps[:, 0:2 * n].rearrange("p (b k) -> p b k", b=2)
                dg = sv[:, :, t * P:(t + 1) * P]
                st.do(tt(dg, dg, causal[:, :].unsqueeze(1).to_broadcast([P, 2, P]), ALU.add))
                o = 32 + 8 * (h % 2) + 4 * t
                nc.vector.tensor_reduce(stat[:, o:o + 2], sv, AX, ALU.max, negate=True).then_inc(neg_max, 1)

            def soft_out(h, t):
                n = (t + 1) * P
                o = 32 + 8 * (h % 2) + 4 * t
                wait_drained(v, ("s", h, t))
                s2 = stat[:, o + 2:o + 4]
                st.do(nc.vector.reciprocal(s2, s2))
                st.do(tt(s2, s2, gv[:, t, h, 1:3], ALU.mult))
                pv = prob[:, h % 2, t, 0:2 * n].rearrange("p (b k) -> p b k", b=2)
                tt(pv, pv, s2.unsqueeze(2).to_broadcast([P, 2, n]), ALU.mult).then_inc(prob_ready, 1)

            def evac_pU(h):
                ps = wait_filled(v, ("pT", h, 1))
                drained(cp(probT[:, h % 2, :, :, P:S], ps[:, :].rearrange("p (b k q) -> p b k q", b=2, k=2)), ("pT", h, 1))

            soft_in(0, 0)
            soft_in(0, 1)
            for h in range(HEADS):
                soft_out(h, 0)
                soft_out(h, 1)
                if h + 1 < HEADS:
                    soft_in(h + 1, 0)
                    soft_in(h + 1, 1)
                evac_pU(h)
                if h == 4:
                    v.wait_ge(stat_ready, 1)
                    for c in range(CC):
                        st.mark(tt(oT[:, c, :], oT[:, c, :], scr[:, 1, :], ALU.mult))
                    st.wait()
                    for c in range(CC):
                        ts(oT[:, c, :], oT[:, c, :], cols[:, C_CG + c:C_CG + c + 1], cols[:, C_CN + c:C_CN + c + 1],
                           ALU.mult, ALU.add).then_inc(convn_ready, 1)
                if h == 5:
                    for c in range(CC):
                        v.wait_ge(convt_ready, c + 1)
                        st.mark(stt(out=oT[:, c, :], in0=aT[:, c, PAD:PAD + S], scalar=1.0, in1=oT[:, c, :], op0=ALU.add, op1=ALU.mult))
                    st.wait()
                    for c in range(CC):
                        ts(oT[:, c, :], oT[:, c, :], 0.5, None, ALU.mult).then_inc(a_out, 1)

            for L in range(DEPTH):
                if L == 1:
                    for c in range(KC):
                        pch = wait_filled(v, ("odc", c))
                        v.wait_ge(od_c, c + 1)
                        ub = aT[:, c % 2, PAD - 2:PAD + S]
                        st.do(tt(aT[:, c % 2, PAD:PAD + S], scr[:, c % 2, :], pch[:, S:2 * S], ALU.mult))
                        w = [cols[:, C_OD + 8 * k + c:C_OD + 8 * k + c + 1] for k in range(3)]
                        drained(ts(u[:, :], ub[:, 2:2 + S], w[2], None, ALU.mult), ("odc", c))
                        wait_drained(v, ("odc", c))
                        for k in (1, 0):
                            st.do(stt(out=u[:, :], in0=ub[:, k:k + S], scalar=w[k], in1=u[:, :], op0=ALU.mult, op1=ALU.add))
                        ps = wait_filled(v, ("odb", c))
                        drained(tt(oT[:, c, :], u[:, :], ps[:, 0:S], ALU.mult), ("odb", c))
                norm_dve(st, v, 3 * L)

                def x_in(h):
                    ps = wait_filled(v, ("xs", L, h))
                    o = 32 + 8 * (h % 2)
                    nc.vector.tensor_reduce(stat[:, o:o + 2], ps[:, :].rearrange("p (t k) -> p t k", t=2), AX, ALU.max, negate=True).then_inc(neg_max, 1)

                def x_out(h):
                    o = 32 + 8 * (h % 2)
                    wait_drained(v, ("xs", L, h))
                    s2 = stat[:, o + 2:o + 4]
                    st.do(nc.vector.reciprocal(s2, s2))
                    pv = prob[:, h % 2, :, 0:S]
                    tt(pv, pv, s2.unsqueeze(2).to_broadcast([P, 2, S]), ALU.mult).then_inc(prob_ready, 1)

                x_in(0)
                for h in range(XH):
                    x_out(h)
                    if h + 1 < XH:
                        x_in(h + 1)
                    ps = wait_filled(v, ("xp", L, h))
                    drained(cp(probT[:, h % 2, 0, :, :], ps[:, :].rearrange("p (m s) -> p m s", m=2)), ("xp", L, h))
                norm_dve(st, v, 3 * L + 1)

                ps = wait_filled(v, ("lg", L))
                v.wait_ge(bias_loaded, 32)
                drained(tt(lg[:, :, :], ps[:, 0:128].rearrange("p (t n) -> p t n", t=TT)[:, :, 0:NG + NE],
                           rbias[:, L, :].unsqueeze(1).to_broadcast([P, TT, NG + NE]), ALU.add), ("lg", L))
                wait_drained(v, ("lg", L))
                st.do(cp(g8[:, :, 0:NG], lg[:, :, 0:NG]))
                for t in range(TT):
                    st.mark(nc.vector.max(top[:, t, 0, :], g8[:, t, :]))
                st.wait()
                for t in range(TT):
                    st.mark(nc.vector.max_index(topi[:, t, 0, :], top[:, t, 0, :], g8[:, t, :]))
                st.mark(ts(rs[:, 0, :], top[:, :, 0, 0], -1.0, None, ALU.mult))
                st.wait()
                cp(topf[:, :, 0, :], topi[:, :, 0, :]).then_inc(gexp_in, 1)
                v.wait_ge(gexp_in, L + 1)
                st.do(tt(ohg[:, :, :], iota[:, 0:NG].unsqueeze(1).to_broadcast([P, TT, NG]),
                         topf[:, :, 0, 0:1].to_broadcast([P, TT, NG]), ALU.is_equal))
                ev = lg[:, :, NG:NG + NE].rearrange("p t (g e) -> p t g e", g=NG)
                for t in range(TT):
                    st.mark(tt(etmp[:, t, :, :], ev[:, t, :, :], ohg[:, t, :].unsqueeze(2).to_broadcast([P, NG, EPG]), ALU.mult))
                st.wait()
                for t in range(TT):
                    st.mark(nc.vector.tensor_reduce(esel[:, t, :], etmp[:, t, :, :].rearrange("p g e -> p e g"), AX, ALU.add))
                st.wait()
                for t in range(TT):
                    st.mark(nc.vector.max(top[:, t, 1, :], esel[:, t, :]))
                st.wait()
                for t in range(TT):
                    st.mark(nc.vector.max_index(topi[:, t, 1, :], top[:, t, 1, :], esel[:, t, :]))
                st.wait()
                tt(rs[:, 2, :], top[:, :, 1, 1], top[:, :, 1, 0], ALU.subtract).then_inc(eexp_in, 1)
                st.do(cp(topf[:, :, 1, :], topi[:, :, 1, :]))
                for m in range(2):
                    st.mark(tt(e01[:, m, :, :], iota[:, 0:EPG].unsqueeze(1).to_broadcast([P, TT, EPG]),
                               topf[:, :, 1, m:m + 1].to_broadcast([P, TT, EPG]), ALU.is_equal))
                st.wait()
                st.do(tt(esel[:, :, :], e01[:, 0, :, :], e01[:, 1, :, :], ALU.add))
                mk = mask[:, :, :].rearrange("p t (g e) -> p t g e", g=NG)
                for t in range(TT):
                    ins = tt(mk[:, t, :, :], ohg[:, t, :].unsqueeze(2).to_broadcast([P, NG, EPG]),
                             esel[:, t, :].unsqueeze(1).to_broadcast([P, NG, EPG]), ALU.mult)
                    if t == 0:
                        st.mark(ins)
                ins.then_inc(mask_ready, 1)
                v.wait_ge(gexp, L + 1)
                v.wait_ge(eexp, L + 1)
                st.do(ts(rs[:, 4, :], rs[:, 3, :], 1.0, None, ALU.add))
                st.do(tt(rs[:, 4, :], rs[:, 4, :], rs[:, 1, :], ALU.mult))
                st.do(nc.vector.reciprocal(rs[:, 4, :], rs[:, 4, :]))
                st.do(tt(rs[:, 5, :], rs[:, 4, :], rs[:, 3, :], ALU.mult))
                for m in range(2):
                    st.mark(tt(e01[:, m, :, :], e01[:, m, :, :], rs[:, 4 + m, :].unsqueeze(2).to_broadcast([P, TT, EPG]), ALU.mult))
                st.wait()
                v.wait_ge(mask_ready, L + 1)
                st.do(tt(esel[:, :, :], e01[:, 0, :, :], e01[:, 1, :, :], ALU.add))
                for t in range(TT):
                    st.mark(tt(gate[:, t, 0:NE].rearrange("p (g e) -> p g e", g=NG), ohg[:, t, :].unsqueeze(2).to_broadcast([P, NG, EPG]),
                               esel[:, t, :].unsqueeze(1).to_broadcast([P, NG, EPG]), ALU.mult))
                ps = wait_filled(v, ("pos", L))
                pv = ps[:, 0:2 * NE].rearrange("p (t e) -> p t e", t=TT)
                st.do(stt(out=place[:, :, 0:NE], in0=pv, scalar=1.0, in1=mask[:, :, :], op0=ALU.add, op1=ALU.mult))
                st.do(ts(place[:, :, 0:NE], place[:, :, 0:NE], -1.0, None, ALU.add))
                drained(nc.vector.tensor_reduce(most[:, L:L + 1], ps[:, 64:64 + NE], AX, ALU.max), ("pos", L))
                wait_drained(v, ("pos", L))
                cp(mosti[:, :], most[:, L:L + 1]).then_inc(count_ready, 1)

                def build(fam, pair):
                    tt(disp[:, :, :, :], iota[:, :].unsqueeze(1).unsqueeze(1).to_broadcast([P, TT, 2, CAP]),
                       place[:, :, bass.ds(pair * 2, 2)].unsqueeze(3).to_broadcast([P, TT, 2, CAP]), ALU.is_equal).then_inc(fam.disp_built, 1)

                def weight(fam, pair):
                    for j in range(2):
                        ins = tt(dispg[:, j, :, :, :], disp[:, :, j, :].unsqueeze(2).to_broadcast([P, TT, 2, CAP]),
                                 gate[:, :, bass.ds(pair * 2 + j, 1)].unsqueeze(3).to_broadcast([P, TT, 2, CAP]), ALU.mult)
                    ins.then_inc(fam.disp_gated, 1)

                def take(fam, n, h):
                    v.wait_ge(fam.gather_done, n * 2 + (h + 1))
                    cp(xgT[:, 4 * h:4 * h + 4, :], bG_(h)).then_inc(fam.gathered, 1)

                def bG_(h):
                    return banks[7][:, :].rearrange("p (k s) -> p k s", k=4)

                def expert_pass(fam, q, extra):
                    nc.vector.memset(comb[:, 1, :], 0.0).then_inc(fam.comb_ready, 1)
                    nc.vector.memset(y[:, 1, :], 0.0).then_inc(fam.y_ready, 1)
                    build(fam, 0)
                    v.wait_ge(fam.disp_built, q * 17 + 1)
                    weight(fam, 0)
                    take(fam, q * 17, 0)
                    take(fam, q * 17, 1)
                    with v.Fori(0, PAIRS) as i:
                        v.wait_ge(fam.gather_done, (q * 17 + i) * 2 + 2)
                        v.wait_ge(fam.disp_gated, q * 17 + i + 1)
                        build(fam, i + 1)
                        for j in range(2):
                            e1 = q * NE + i * 2 + (j + 1)
                            v.wait_ge(fam.tanh_done, e1)
                            stt(out=u[:, :], in0=th[:, :], scalar=1.0, in1=banks[4][:, 0:S], op0=ALU.add, op1=ALU.mult).then_inc(fam.glu_done, 1)
                            v.wait_ge(fam.glu_done, e1 + extra)
                            stt(out=hid[:, :], in0=u[:, :], scalar=0.5, in1=banks[4][:, S:2 * S], op0=ALU.mult, op1=ALU.mult).then_inc(fam.hidden_ready, 1)
                            if j == 1:
                                take(fam, q * 17 + i + 1, 0)
                                v.wait_ge(fam.comb_done, e1)
                                v.wait_ge(fam.disp_built, q * 17 + i + 2)
                                weight(fam, i + 1)
                                take(fam, q * 17 + i + 1, 1)

                st.wait()
                if L:
                    v.wait_ge(passes_done[L - 1], 1)
                expert_pass(main, L, 0)
                v.wait_ge(count_ready, L + 1)
                longest = v.value_load(mosti[0:1, 0:1], min_val=0, max_val=S)
                with v.Fori(0, PASSES - 1) as q:
                    with v.If(longest > q * CAP + CAP):
                        v.wait_ge(passes_done[L], q + 1)
                        ts(place[:, :, 0:NE], place[:, :, 0:NE], -float(CAP), None, ALU.add).then_inc(over[L].glu_done, 1)
                        v.wait_ge(over[L].glu_done, q * (NE + 1) + 1)
                        expert_pass(over[L], q, q + 1)
                norm_dve(st, v, 3 * L + 2)

        @block.scalar
        def _(a):
            st = Steps(a, act_step)
            act, cp = nc.scalar.activation, nc.scalar.copy
            for t in range(TT):
                ps = wait_filled(a, (("x",), t, 0))
                drained(cp(xT[:, 0:4, t * P:(t + 1) * P], ps[:, :].rearrange("p (k s) -> p k s", k=4)), (("x",), t, 0))
            for c in range(CC):
                ps = wait_filled(a, ("a", c))
                if c >= 2:
                    wait_drained(a, ("a", c - 2))
                act(scr[:, c % 2, :], ps[:, S:2 * S], ACT.Tanh, scale=0.5).then_inc(sig_ready, 1)
            for t in range(TT):
                ps = wait_filled(a, (("mem",), t, 0))
                drained(cp(memT[:, 0:4, t * P:(t + 1) * P], ps[:, :].rearrange("p (k s) -> p k s", k=4)), (("mem",), t, 0))
            for j in range(2):
                ps = wait_filled(a, ("q", j))
                drained(nc.scalar.mul(qT[:, 2 * j:2 * j + 2, :], ps[:, :].rearrange("p (c s) -> p c s", c=2), HD ** -0.5), ("q", j))
            for g in range(2):
                ps = wait_filled(a, ("k", g))
                drained(cp(kT[:, g, :], ps[:, :]), ("k", g))
            for t in range(TT):
                ps = wait_filled(a, ("v", t))
                cp(v_sb[:, t, :, :], ps[:, 0:2 * P].rearrange("p (b n) -> p b n", b=2))
                ins = act(gates[:, t, :], ps[:, 2 * P:2 * P + 24], ACT.Tanh, scale=0.5)
                drained(ins, ("v", t))
            for j in range(4):
                ps = wait_filled(a, ("mk", j))
                drained(nc.scalar.mul(mem_kT[:, 2 * j:2 * j + 2, :], ps[:, :].rearrange("p (c s) -> p c s", c=2), (D // XH) ** -0.5), ("mk", j))
            wait_drained(a, ("ch",))
            act(gtmp[:, :, 0:2 * NCMP], gtmp[:, :, 0:2 * NCMP], ACT.Tanh, scale=GELU_B).then_inc(gelu_tanh, 1)
            for h in range(2):
                for t in range(TT):
                    ps = wait_filled(a, ("mv", t, h))
                    drained(cp(mem_v[:, t, h * 512:(h + 1) * 512], ps[:, :]), ("mv", t, h))
            ps = wait_filled(a, ("c2",))
            nc.scalar.mul(k_cmpT[:, :, 0:NCMP], ps[:, 0:32].rearrange("p (g n) -> p g n", g=2)[:, :, 0:NCMP], 0.5)
            drained(nc.scalar.mul(v_cmp[0:NCMP, :, :], ps[0:NCMP, 64:64 + 2 * HD].rearrange("p (g n) -> p g n", g=2), 0.5), ("c2",))
            a.wait_ge(cmax, 1)
            act(pc[:, :, :, 0:NCMP], pc[:, :, :, 0:NCMP], ACT.Exp).then_inc(cexp, 1)

            def exps(h, t):
                n = (t + 1) * P
                o = 32 + 8 * (h % 2) + 4 * t
                a.wait_ge(neg_max, 2 * h + t + 1)
                if h >= 2:
                    wait_filled(a, ("pT", h - 2, t))
                ps = banks[bank_of[("s", h, t)][0]]
                act(prob[:, h % 2, t, 0:n], ps[:, 0:n], ACT.Exp, bias=stat[:, o:o + 1], accum_out=stat[:, o + 2:o + 3])
                drained(act(prob[:, h % 2, t, n:2 * n], ps[:, n:2 * n], ACT.Exp, bias=stat[:, o + 1:o + 2], accum_out=stat[:, o + 3:o + 4]), ("s", h, t))

            def evac_pT(h):
                ps = wait_filled(a, ("pT", h, 0))
                st.mark(cp(probT[:, h % 2, :, 0, 0:P], ps[:, 0:2 * P].rearrange("p (b q) -> p b q", b=2)))
                drained(cp(pcT[:, h % 2, :], ps[0:16, 2 * P:4 * P]), ("pT", h, 0))

            exps(0, 0)
            exps(0, 1)
            for h in range(HEADS):
                if h + 1 < HEADS:
                    exps(h + 1, 0)
                    exps(h + 1, 1)
                evac_pT(h)
                if h % 2 == 0 and h >= 2:
                    c = h // 2 - 1
                    ps = wait_filled(a, ("o", c))
                    drained(cp(oT[:, CC + c, :], ps[:, 0:S]), ("o", c))
                if h == 3:
                    ps = wait_filled(a, ("cvar",))
                    drained(cp(scr[:, 0, :], ps[:, 0:S]), ("cvar",))
                if h == 4:
                    for c in range(CC):
                        a.wait_ge(convn_ready, c + 1)
                        act(aT[:, c, PAD:PAD + S], oT[:, c, :], ACT.Tanh, scale=0.5).then_inc(convt_ready, 1)
            ps = wait_filled(a, ("o", CC - 1))
            drained(cp(oT[:, 2 * CC - 1, :], ps[:, 0:S]), ("o", CC - 1))

            for L in range(DEPTH):
                if L == 1:
                    for c in range(KC):
                        ps = wait_filled(a, ("odc", c))
                        if c >= 2:
                            wait_drained(a, ("odc", c - 2))
                        cp(scr[:, c % 2, :], ps[:, 0:S]).then_inc(od_c, 1)
                if L == 0:
                    a.wait_ge(small_loaded, 16 * 12)
                norm_act(a, 3 * L)
                for j in range(4):
                    ps = wait_filled(a, ("xq", L, j))
                    drained(cp(qxT[:, 2 * j:2 * j + 2, :], ps[:, :].rearrange("p (c s) -> p c s", c=2)), ("xq", L, j))

                def xexps(h):
                    o = 32 + 8 * (h % 2)
                    a.wait_ge(neg_max, 2 * HEADS + L * XH + h + 1)
                    if h >= 2:
                        wait_filled(a, ("xp", L, h - 2))
                    ps = banks[bank_of[("xs", L, h)][0]]
                    act(prob[:, h % 2, 0, 0:S], ps[:, 0:S], ACT.Exp, bias=stat[:, o:o + 1], accum_out=stat[:, o + 2:o + 3])
                    drained(act(prob[:, h % 2, 1, 0:S], ps[:, S:2 * S], ACT.Exp, bias=stat[:, o + 1:o + 2], accum_out=stat[:, o + 3:o + 4]), ("xs", L, h))

                def evac_xo(h):
                    ps = wait_filled(a, ("xo", L, h))
                    drained(cp(oT[:, 2 * h:2 * h + 2, :], ps[:, :].rearrange("p (c s) -> p c s", c=2)), ("xo", L, h))

                xexps(0)
                for h in range(XH):
                    if h + 1 < XH:
                        xexps(h + 1)
                    if h > 0:
                        evac_xo(h - 1)
                evac_xo(XH - 1)
                norm_act(a, 3 * L + 1)
                a.wait_ge(gexp_in, L + 1)
                for t in range(TT):
                    ins = act(esum[:, t, :], g8[:, t, 0:NG], ACT.Exp, bias=rs[:, 0, t:t + 1], accum_out=rs[:, 1, t:t + 1])
                    if t == 0:
                        st.mark(ins)
                ins.then_inc(gexp, 1)
                a.wait_ge(eexp_in, L + 1)
                act(rs[:, 3, :], rs[:, 2, :], ACT.Exp).then_inc(eexp, 1)

                def expert_pass(fam, q):
                    with a.Fori(0, PAIRS) as i:
                        for j in range(2):
                            e1 = q * NE + i * 2 + (j + 1)
                            a.wait_ge(fam.hid_done, e1)
                            act(th[:, :], banks[4][:, 0:S], ACT.Tanh, scale=0.5).then_inc(fam.tanh_done, 1)
                            a.wait_ge(fam.comb_done, e1)
                            cp(comb[:, j, :], banks[5][:, 0:S]).then_inc(fam.comb_ready, 1)
                            a.wait_ge(fam.hidT_done, e1)
                            cp(hidT[:, :, :], banks[6][:, 0:S].rearrange("p (c s) -> p c s", c=2)).then_inc(fam.hidT_ready, 1)
                            a.wait_ge(fam.y_done, e1)
                            cp(y[:, j, :], banks[5][:, :]).then_inc(fam.y_ready, 1)

                expert_pass(main, L)
                a.wait_ge(count_ready, L + 1)
                longest = a.value_load(mosti[0:1, 0:1], min_val=0, max_val=S)
                with a.Fori(0, PASSES - 1) as q:
                    with a.If(longest > q * CAP + CAP):
                        expert_pass(over[L], q)
                if L + 1 < DEPTH:
                    norm_act(a, 3 * L + 2)

        @block.gpsimd
        def _(g):
            st = Steps(g, pool_step)
            ms, sel = nc.gpsimd.memset, nc.gpsimd.affine_select

            st.do(ms(ident[:, :], 0.0))
            sel(out=ident[:, :], in_=ident[:, :], compare_op=ALU.not_equal, fill=1.0, base=0,
                pattern=[[-1, P]], channel_multiplier=1).then_inc(consts_ready, 1)
            g.wait_ge(consts_ready, 1)
            def small(dst, src):
                g.dma_start(dst, src).then_inc(small_loaded, 16)

            small(w2c[:, 0, :, :], T["ev_cmp_w2_k"][0].rearrange("(h p) d -> p h d", p=P))
            small(w2c[:, 1, :, :], T["ev_cmp_w2_v"][0].rearrange("(h p) d -> p h d", p=P))
            for L in range(DEPTH):
                small(wr[:, L, :, 0:NG], T["moe_wg"][L].rearrange("(p k) g -> p k g", k=KC))
                small(wr[:, L, :, NG:NG + NE], T["moe_we"][L].rearrange("(p k) g e -> p k (g e)", k=KC))
            for m in range(2):
                for s, n in enumerate(("ln_mix", "ln_xa", "ln_ffn")):
                    dst = lngT[:, :, m, :].rearrange("p (l s) k -> p s l k", s=3)[:, s, :, :]
                    g.dma_start(dst, T[f"{n}_{'gb'[m]}"].rearrange("l (p k) -> p l k", k=KC)).then_inc(small_loaded, 16)
            g.dma_start(rbias[:, :, 0:NG], T["moe_bg"].unsqueeze(0).to_broadcast([P, DEPTH, NG])).then_inc(bias_loaded, 16)
            g.dma_start(rbias[:, :, NG:NG + NE], T["moe_be"].rearrange("l g e -> l (g e)").unsqueeze(0).to_broadcast([P, DEPTH, NE])).then_inc(bias_loaded, 16)
            ms(ones[:, :], 1.0)
            ms(onesc[:, :], 1.0 / CONV_CH)
            ms(zero16[:, :], 0.0)
            ms(half[:, :], -0.5)
            nc.gpsimd.iota(iota[:, :], pattern=[[1, CAP]], base=0, channel_multiplier=0, allow_small_or_imprecise_dtypes=True)
            ms(tri[:, :], 1.0)
            ms(causal[:, :], 0.0)
            ms(cmask[:, :, :], 1.0)
            st.do(ms(cbias[:, :, :], 0.0))
            sel(out=tri[:, :], in_=tri[:, :], compare_op=ALU.is_gt, fill=0.0, base=0, pattern=[[1, P]], channel_multiplier=-1)
            sel(out=causal[:, :], in_=causal[:, :], compare_op=ALU.is_ge, fill=NEG, base=0, pattern=[[-1, P]], channel_multiplier=1)
            pat = [[P, TT], [-CMP_STRIDE, 16]]
            sel(out=cmask[:, :, :], in_=cmask[:, :, :], compare_op=ALU.is_ge, fill=0.0, base=-31, pattern=pat, channel_multiplier=1)
            sel(out=cbias[:, :, :], in_=cbias[:, :, :], compare_op=ALU.is_ge, fill=NEG, base=-31, pattern=pat, channel_multiplier=1).then_inc(consts_ready, 1)

            def load_gb(i):
                n = ("ln_mix", "ln_xa", "ln_ffn")[i % 3]
                for m in range(2):
                    g.dma_start(gb[:, m, :], T[f"{n}_{'gb'[m]}"][i // 3:i // 3 + 1, :].to_broadcast([P, D])).then_inc(gb_loaded, 16)

            def norm(i):
                for t in range(TT):
                    g.wait_ge(ln_stats, 2 * i + t + 1)
                    st.do(nc.gpsimd.tensor_scalar(vare[:, t, :], mv[:, t, 1:2], EPS, None, ALU.add))
                    nc.gpsimd.tensor_tensor(rstd[:, t, :], vare[:, t, :], half[:, t:t + 1], ALU.pow).then_inc(ln_rstd, 1)

            wait_filled(g, (("mem",), 0, 1))
            wait_filled(g, (("mem",), 1, 1))
            load_gb(0)
            wait_drained(g, ("cvar",))
            st.do(nc.gpsimd.tensor_scalar(scr[:, 0, :], scr[:, 0, :], EPS, None, ALU.add))
            nc.gpsimd.tensor_tensor(scr[:, 1, :], scr[:, 0, :], half[:, :], ALU.pow).then_inc(stat_ready, 1)
            for i in range(LN_COUNT):
                norm(i)
                if i + 1 < LN_COUNT:
                    g.wait_ge(x_ready, 2 * i + 2)
                    load_gb(i + 1)


_OUTS = [((1, S, D), "float32")]


def kernel(**inputs):
    import numpy as _np
    import concourse.bacc as _bacc
    from concourse import mybir as _mybir
    from concourse.bass_utils import run_bass_kernel_spmd as _run

    nc = _bacc.Bacc("TRN2", target_bir_lowering=False, num_devices=1)
    arrays, tensors = {}, {}
    for name, value in inputs.items():
        a = _np.ascontiguousarray(value)
        arrays[f"in_{name}_dram"] = a
        tensors[name] = nc.dram_tensor(f"in_{name}_dram", a.shape, _mybir.dt.from_np(a.dtype), kind="ExternalInput").ap()
    shape, dtype = _OUTS[0]
    out = nc.dram_tensor("out_0_dram", shape, _mybir.dt.from_np(_np.dtype(dtype)), kind="ExternalOutput").ap()
    program(nc, tensors, out)
    r = _run(nc, [arrays], core_ids=[0])
    return r.results[0]["out_0_dram"]
```

```python
from contextlib import ExitStack

import concourse.bass as bass
from concourse import mybir

F32 = mybir.dt.float32
BF16 = mybir.dt.bfloat16
U32 = mybir.dt.uint32
I32 = mybir.dt.int32
ACT = mybir.ActivationFunctionType
ALU = mybir.AluOpType
AX = mybir.AxisListType.X

P = 128
D = 1024
S = 256
TT = S // P
KC = D // P
DEPTH = 2
CONV_CH = D // 2
CC = CONV_CH // P
TAPS = 31
PAD = TAPS - 1
HEADS = 8
HD = (D // 2) // HEADS
CMP_STRIDE = 16
NCMP = (S - 32) // CMP_STRIDE + 1
XH = 4
NG = 4
EPG = 8
NE = NG * EPG
CAP = 64
PAIRS = NE // 2
ROUNDS = S // CAP
RING = 6
ALPHA = (2 * DEPTH) ** 0.25
EPS = 1e-5
NEG = -1e30
GELU_A = 0.044715
GELU_B = 0.7978845608028654
LN_COUNT = 3 * DEPTH
C_CB, C_CG, C_CN, C_OD, C_PK, C_PV, C_ALL = 0, 4, 8, 12, 36, 52, 68


class Steps:

    def __init__(self, eng, sem):
        self.eng, self.sem, self.n = eng, sem, 0

    def mark(self, ins):
        ins.then_inc(self.sem, 1)
        self.n += 1
        return self.n

    def wait(self, n=None):
        self.eng.wait_ge(self.sem, self.n if n is None else n)

    def do(self, ins):
        self.mark(ins)
        self.wait()


def program(nc, T, out):
    ctx = ExitStack()
    with ctx:
        def sb(name, shape, dt=F32):
            return ctx.enter_context(nc.sbuf_tensor(name, shape, dt))

        def sem(name):
            return ctx.enter_context(nc.semaphore(name))

        ring = sb("ring", [P, RING, 4096])
        x = sb("x", [P, TT, D])
        xT = sb("xT", [P, KC, S])
        memT = sb("memT", [P, KC, S])
        qxT = memT
        oT = sb("oT", [P, KC, S])
        mem_kT = sb("mem_kT", [P, KC, S])
        mem_v = sb("mem_v", [P, TT, D])
        gb = sb("gb", [P, 2, D])
        qT = sb("qT", [P, CC, S])
        aT = sb("aT", [P, CC, PAD + S])
        kT = sb("kT", [P, 2, 2 * S])
        xgT = kT[:, :, :].rearrange("p a b -> p (a b)").rearrange("p (k s) -> p k s", k=KC)
        blocks = sb("blocks", [P, 2, 16, 2, NCMP])
        v_sb = sb("v_sb", [P, TT, 2, P])
        prob = sb("prob", [P, 2, 2, 2 * S])
        probT = sb("probT", [P, 2, 2, TT, S])
        pc = sb("pc", [P, TT, HEADS, 16])
        pcT = sb("pcT", [16, 2, S])
        k_cmpT = sb("k_cmpT", [P, 2, 16])
        v_cmp = sb("v_cmp", [16, 2, HD])
        ghid = sb("ghid", [P, 4, 32])
        gtmp = sb("gtmp", [P, 4, 32])
        w2c = sb("w2c", [P, 2, 2, HD])
        gates = sb("gates", [P, TT, 24])
        stat = sb("stat", [P, 64])
        scr = sb("scr", [P, 2, S])
        ident = sb("ident", [P, P])
        tri = sb("tri", [P, P])
        ones = sb("ones", [P, P])
        onesc = sb("onesc", [P, P])
        causal = sb("causal", [P, P])
        cmask = sb("cmask", [P, TT, 16])
        cbias = sb("cbias", [P, TT, 16])
        zero16 = sb("zero16", [P, 512], BF16)
        half = sb("half", [P, S])
        iota = sb("iota", [P, CAP])
        round_caps = sb("round_caps", [P, ROUNDS - 1])
        rows1 = sb("rows1", [P, P])
        rows2 = sb("rows2", [C_ALL, P])
        cw = sb("cw", [P, TAPS * CC])
        cols = sb("cols", [P, C_ALL])
        lngT = sb("lngT", [P, LN_COUNT, 2, KC])
        wr = sb("wr", [P, DEPTH, KC, NG + NE])
        rbias = sb("rbias", [P, DEPTH, NG + NE])
        lg = sb("lg", [P, TT, NG + NE])
        g8 = sb("g8", [P, TT, 8])
        top = sb("top", [P, TT, 2, 8])
        topi = sb("topi", [P, TT, 2, 8], U32)
        topf = sb("topf", [P, TT, 2, 8])
        ohg = sb("ohg", [P, TT, NG])
        esel = sb("esel", [P, TT, 8])
        etmp = sb("etmp", [P, TT, NG, EPG])
        e01 = sb("e01", [P, 2, TT, EPG])
        rs = sb("rs", [P, 8, TT])
        mask = sb("mask", [P, TT, NE])
        place = sb("place", [P, TT, NE + 2])
        gate = sb("gate", [P, TT, NE + 2])
        counts = sb("counts", [P, 4, PAIRS])
        rounds = sb("rounds", [P, PAIRS, 2], I32)
        shifted = sb("shifted", [P, TT, 2])
        def carve(t, shapes):
            flat = t[:].rearrange({3: "p a b -> p (a b)", 4: "p a b c -> p (a b c)", 5: "p a b c d -> p (a b c d)"}[len(t.shape)])
            at, found = 0, []
            for names, sizes in shapes:
                n = 1
                for x_ in sizes:
                    n *= x_
                v_ = flat[:, at:at + n]
                at += n
                if len(sizes) > 1:
                    v_ = v_.rearrange(f"p ({names}) -> p {names}", **dict(zip(names.split(), sizes)))
                found.append(v_)
            return found

        hid, hidT, th, u512 = carve(probT, [("n", (512,)), ("c s", (4, P)), ("n", (512,)), ("n", (512,))])
        y, comb, disp, dispg = carve(prob, [
            ("n", (D,)),
            ("n", (S,)),
            ("t e s", (TT, 2, CAP)),
            ("t e s", (TT, 2, CAP))])
        more_disp, more_dispg = carve(blocks, [("t e s", (TT, 2, CAP)), ("t e s", (TT, 2, CAP))])
        (more_xgT,) = carve(qT, [("k s", (KC, P))])
        (more_y,) = carve(aT, [("n", (D,))])
        more_comb = scr[:, 0, :]
        u = sb("u", [P, S])
        bn = sb("bn", [P, TT, 2, 6])
        mv = sb("mv", [P, TT, 2])
        rstd = sb("rstd", [P, TT, 1])
        esum = sb("esum", [P, TT, NG])
        vare = sb("vare", [P, TT, 1])

        banks = [ctx.enter_context(nc.psum_tensor(f"bank{i}", [P, 512], F32)) for i in range(8)]

        loaded = [sem(f"loaded{i}") for i in range(RING)]
        weights_used = sem("weights_used")
        bank_filled = [sem(f"bank_filled{i}") for i in range(8)]
        bank_drained = [sem(f"bank_drained{i}") for i in range(8)]
        x_loaded = sem("x_loaded")
        mem_loaded = sem("mem_loaded")
        rows_loaded = sem("rows_loaded")
        small_loaded = sem("small_loaded")
        bias_loaded = sem("bias_loaded")
        gb_loaded = sem("gb_loaded")
        stored = sem("stored")
        consts_ready = sem("consts_ready")
        pool_step = sem("pool_step")
        dve_step = sem("dve_step")
        act_step = sem("act_step")
        sig_ready = sem("sig_ready")
        sig_used = sem("sig_used")
        conv_ready = sem("conv_ready")
        sq_ready = sem("sq_ready")
        stat_ready = sem("stat_ready")
        convn_ready = sem("convn_ready")
        convt_ready = sem("convt_ready")
        a_out = sem("a_out")
        gelu_in = sem("gelu_in")
        gelu_tanh = sem("gelu_tanh")
        gelu_out = sem("gelu_out")
        neg_max = sem("neg_max")
        prob_ready = sem("prob_ready")
        cmax = sem("cmax")
        cexp = sem("cexp")
        cprob = sem("cprob")
        od_c = sem("od_c")
        ln_stats = sem("ln_stats")
        ln_rstd = sem("ln_rstd")
        n_ready = sem("n_ready")
        x_ready = sem("x_ready")
        xT_half = sem("xT_half")
        gexp_in = sem("gexp_in")
        gexp = sem("gexp")
        eexp_in = sem("eexp_in")
        eexp = sem("eexp")
        mask_ready = sem("mask_ready")
        rounds_ready = sem("rounds_ready")
        held_over = sem("held_over")
        shift_done = [sem(f"shift_done{L}") for L in range(DEPTH)]

        class Family:

            def __init__(self, name):
                self.w1_used = sem(f"{name}_w1_used")
                self.hid_done = sem(f"{name}_hid_done")
                self.tanh_done = sem(f"{name}_tanh_done")
                self.glu_done = sem(f"{name}_glu_done")
                self.hidden_ready = sem(f"{name}_hidden_ready")
                self.hidT_done = sem(f"{name}_hidT_done")
                self.hidT_ready = sem(f"{name}_hidT_ready")
                self.comb_done = sem(f"{name}_comb_done")
                self.comb_ready = sem(f"{name}_comb_ready")
                self.y_done = sem(f"{name}_y_done")
                self.y_ready = sem(f"{name}_y_ready")
                self.scattered = sem(f"{name}_scattered")
                self.disp_built = sem(f"{name}_disp_built")
                self.disp_gated = sem(f"{name}_disp_gated")
                self.gather_done = sem(f"{name}_gather_done")
                self.gathered = sem(f"{name}_gathered")

        main = Family("first")
        over = [Family(f"more{L}") for L in range(DEPTH)]

        slot_of, slot_uses, slot_last = {}, [0] * RING, [None] * RING
        order = []
        bank_of, fills, rotation = {}, [0] * 8, [0]
        moe_base = []

        def slot(key):
            return ring[:, slot_of[key][0], :]

        def wait_loaded(eng, key):
            s, n = slot_of[key]
            eng.wait_ge(loaded[s], 16 * n)

        def claim(pe, key, bank=None):
            b = rotation[0] if bank is None else bank
            if bank is None:
                rotation[0] = (b + 1) % 8
            if fills[b]:
                pe.wait_ge(bank_drained[b], fills[b])
            fills[b] += 1
            bank_of[key] = (b, fills[b])
            return banks[b]

        def filled(ins, key):
            ins.then_inc(bank_filled[bank_of[key][0]], 1)

        def wait_filled(eng, key):
            b, n = bank_of[key]
            eng.wait_ge(bank_filled[b], n)
            return banks[b]

        def drained(ins, key):
            ins.then_inc(bank_drained[bank_of[key][0]], 1)

        def wait_drained(eng, key):
            b, n = bank_of[key]
            eng.wait_ge(bank_drained[b], n)

        def load_rounds(eng, pair):
            at_ = rounds[0:1, bass.ds(pair, 1), :] if not isinstance(pair, int) else rounds[0:1, pair:pair + 1, :]
            n = eng.value_load(at_[:, 0, 0:1], min_val=0, max_val=ROUNDS - 1)
            before = eng.value_load(at_[:, 0, 1:2], min_val=0, max_val=8)
            return n, before

        block = ctx.enter_context(nc.Block())

        @block.sync
        def _(sp):
            at = [0]

            def load(key, dst_view, src):
                s = at[0] % RING
                at[0] += 1
                last = slot_last[s]
                if last is not None:
                    sp.wait_ge(last[0], last[1])
                slot_uses[s] += 1
                slot_of[key] = (s, slot_uses[s])
                order.append(key)
                slot_last[s] = (weights_used, len(order))
                sp.dma_start(dst_view(ring[:, s, :]), src).then_inc(loaded[s], 16)

            def load_cols(key, w, c0, n=512):
                load(key, lambda r: r[:, 0:KC * n].rearrange("p (k n) -> p k n", k=KC),
                     w[:, c0:c0 + n].rearrange("(p k) n -> p k n", k=KC))

            def load_out(key, w, c0):
                load(key, lambda r: r.rearrange("p (k n) -> p k n", k=KC),
                     w[:, c0:c0 + 512].rearrange("(k p) n -> p k n", p=P))

            sp.dma_start(x[:, :, :], T["x"][0].rearrange("(t p) d -> p t d", p=P)).then_inc(x_loaded, 16)
            load_cols("av", T["ev_w_in"][0], 0)
            load_cols("ag", T["ev_w_in"][0], 512)
            sp.dma_start(rows1[0:TAPS * CC, :], T["ev_conv_w"][0].rearrange("j (c p) -> (j c) p", p=P)).then_inc(rows_loaded, 16)
            for c, n in ((C_CB, "ev_conv_b"), (C_CG, "ev_cnorm_g"), (C_CN, "ev_cnorm_b")):
                sp.dma_start(rows2[c:c + CC, :], T[n][0].rearrange("(c p) -> c p", p=P)).then_inc(rows_loaded, 16)
            sp.dma_start(rows2[C_OD:C_OD + 24, :], T["od_conv_w"][0].rearrange("j (c p) -> (j c) p", p=P)).then_inc(rows_loaded, 16)
            for c, n in ((C_PK, "ev_cmp_pe_k"), (C_PV, "ev_cmp_pe_v")):
                sp.dma_start(rows2[c:c + 16, :], T[n][0].rearrange("(j l) d -> j (l d)", l=2)).then_inc(rows_loaded, 16)
            sp.dma_start(gb[:, :, :], T["mem"][0].rearrange("(t p) d -> p t d", p=P)).then_inc(mem_loaded, 16)
            load_cols("q", T["ev_w_in"][0], 1024)
            load_cols("kv", T["ev_w_in"][0], 1536)
            load_cols("kw", T["ev_w_in"][0], 2048, 280)
            load_cols("mk0", T["mem_wk"], 0)
            load_cols("mk1", T["mem_wk"], 512)
            for b, n in enumerate(("ev_cmp_w1_k", "ev_cmp_w1_v")):
                load(f"c{b}", lambda r: r.rearrange("p (j n) -> p j n", j=16),
                     T[n][0].rearrange("(j p) n -> p j n", p=P))
            load_cols("mv0", T["mem_wv"], 0)
            load_cols("mv1", T["mem_wv"], 512)

            PARTS = (("moe_w1", "w1_used"), ("moe_w3", "hid_done"), ("moe_w2", "y_done"))

            def expert_weights(name, L, i, j):
                w = T[name][L].rearrange("(i j) a b -> i j a b", j=2)[i, j]
                return w.rearrange("(p k) n -> p (k n)", p=P)

            for L in range(DEPTH):
                if L == 0:
                    load_out("wo_mix0a", T["ev_w_out"][0], 0)
                    load_out("wo_mix0b", T["ev_w_out"][0], 512)
                else:
                    for h in range(2):
                        for part, c0 in (("c", D), ("h", 2 * D), ("b", 0)):
                            load_cols(f"od_{part}{h}", T["od_w_in"][0], c0 + 512 * h)
                    load_out("wo_mix1a", T["od_w_out"][0], 0)
                    load_out("wo_mix1b", T["od_w_out"][0], 512)
                for h in range(2):
                    load_cols(f"xq{L}{h}", T["xa_wq"][L], 512 * h)
                for h in range(2):
                    load_out(f"xo{L}{'ab'[h]}", T["xa_wo"][L], 512 * h)
                for s in range(RING):
                    if slot_last[s] is not None:
                        sp.wait_ge(slot_last[s][0], slot_last[s][1])
                    sp.dma_start(ring[:, s, :], expert_weights(PARTS[s // 2][0], L, 0, s % 2)).then_inc(loaded[s], 16)
                moe_base.append(list(slot_uses))
                sp.wait_ge(rounds_ready, L + 1)
                with sp.Fori(1, PAIRS) as i:
                    n, before = load_rounds(sp, i - 1)
                    with sp.If(n > 0):
                        sp.wait_ge(over[L].scattered, before + n)
                        sp.sem_inc(held_over, 1)
                    for s in range(RING):
                        if s % 2 == 0:
                            sp.wait_ge((main.w1_used, main.hid_done, main.y_done)[s // 2], i + L * PAIRS)
                        sp.dma_start(ring[:, s, :], expert_weights(PARTS[s // 2][0], L, i, s % 2)).then_inc(loaded[s], 16)
                n, before = load_rounds(sp, PAIRS - 1)
                with sp.If(n > 0):
                    sp.wait_ge(over[L].scattered, before + n)
                    sp.sem_inc(held_over, 1)
                for s in range(RING):
                    slot_uses[s] += PAIRS
                    slot_last[s] = ((main.w1_used, main.hid_done, main.y_done)[s // 2], (L + 1) * PAIRS)
                at[0] = 0
            sp.wait_ge(x_ready, 2 * LN_COUNT)
            sp.dma_start(out[0].rearrange("(t p) d -> p t d", p=P), x[:, :, :]).then_inc(stored, 16)
            sp.wait_ge(stored, 16)

        @block.tensor
        def _(pe):
            mm = nc.tensor.matmul
            used = [0]

            def release(ins, key):
                assert order[used[0]] == key, (order[used[0]], key)
                used[0] += 1
                ins.then_inc(weights_used, 1)

            def transposed(key, src):
                for t in range(TT):
                    if key[0] == "n":
                        pe.wait_ge(n_ready, 2 * key[1] + t + 1)
                    for h in range(2):
                        ps = claim(pe, (key, t, h))
                        for k in range(4):
                            cols_ = src[:, t, :].rearrange("p (q k) -> p k q", k=KC)[:, 4 * h + k, :]
                            ins = nc.tensor.transpose(ps[:, k * P:(k + 1) * P], cols_, ident[:, :])
                        filled(ins, (key, t, h))

            def wait_xT(key):
                for t in range(TT):
                    for h in range(2):
                        wait_drained(pe, (key, t, h))

            def by_weight(key, wkey, c0, rhs, ps, last):
                w = slot(wkey)[:, 0:KC * last].rearrange("p (k n) -> p k n", k=KC)
                for k in range(KC):
                    ins = mm(ps, w[:, k, c0:c0 + P], rhs[:, k, :], start=(k == 0), stop=(k == KC - 1))
                return ins

            def out_projection(name, i):
                for h in range(2):
                    wkey = f"{name}{'ab'[h]}"
                    wait_loaded(pe, wkey)
                    w = slot(wkey).rearrange("p (k n) -> p k n", k=KC)
                    for t in range(TT):
                        ps = claim(pe, ("f", i, t, h))
                        for k in range(KC):
                            ins = mm(ps[:, :], oT[:, k, t * P:(t + 1) * P], w[:, k, :], start=(k == 0), stop=(k == KC - 1))
                        filled(ins, ("f", i, t, h))
                    pe.wait_ge(bank_filled[bank_of[("f", i, TT - 1, h)][0]], bank_of[("f", i, TT - 1, h)][1])
                    release(pe.nop(), wkey)

            def signal_release(key, tile):
                b, n = bank_of[tile]
                pe.wait_ge(bank_filled[b], n)
                release(pe.nop(), key)

            pe.wait_ge(consts_ready, 1)
            pe.wait_ge(x_loaded, 16)
            transposed(("x",), x)
            pe.wait_ge(rows_loaded, 16 * 7)
            ps = claim(pe, ("cols",))
            nc.tensor.transpose(ps[:, 0:TAPS * CC], rows1[0:TAPS * CC, :], ident[0:TAPS * CC, 0:TAPS * CC])
            filled(nc.tensor.transpose(ps[:, 128:128 + C_ALL], rows2[0:C_ALL, :], ident[0:C_ALL, 0:C_ALL]), ("cols",))

            wait_xT(("x",))
            wait_loaded(pe, "av")
            wait_loaded(pe, "ag")
            for c in range(CC):
                ps = claim(pe, ("a", c))
                by_weight(None, "av", c * P, xT, ps[:, 0:S], 512)
                ins = by_weight(None, "ag", c * P, xT, ps[:, S:2 * S], 512)
                filled(ins, ("a", c))
            signal_release("av", ("a", CC - 1))
            release(pe.nop(), "ag")
            pe.wait_ge(mem_loaded, 16)
            transposed(("mem",), gb)

            wait_loaded(pe, "q")
            for j in range(2):
                ps = claim(pe, ("q", j))
                for c in range(2):
                    ins = by_weight(None, "q", (2 * j + c) * P, xT, ps[:, c * S:(c + 1) * S], 512)
                filled(ins, ("q", j))
            signal_release("q", ("q", 1))
            wait_loaded(pe, "kv")
            wait_loaded(pe, "kw")
            wkv = slot("kv").rearrange("p (k n) -> p k n", k=KC)
            wkw = slot("kw")[:, 0:KC * 280].rearrange("p (k n) -> p k n", k=KC)
            for b in range(2):
                ps = claim(pe, ("z", b))
                for g in range(2):
                    c0 = b * P + g * HD
                    for k in range(KC):
                        mm(ps[0:HD, g * S:(g + 1) * S], wkv[:, k, c0:c0 + HD], xT[:, k, :], start=(k == 0), stop=(k == KC - 1))
                        ins = mm(ps[HD:P, g * S:(g + 1) * S - 1], wkv[:, k, c0:c0 + HD], xT[:, k, 1:S], start=(k == 0), stop=(k == KC - 1))
                filled(ins, ("z", b))
            for g in range(2):
                ps = claim(pe, ("k", g))
                for b, (w, c0) in enumerate(((wkv, 2 * P), (wkw, 0))):
                    for k in range(KC):
                        for r in range(2):
                            ins = mm(ps[r * HD:(r + 1) * HD, b * S:(b + 1) * S], w[:, k, c0 + g * HD:c0 + (g + 1) * HD],
                                     xT[:, k, :], start=(k == 0), stop=(k == KC - 1))
                filled(ins, ("k", g))
            for t in range(TT):
                ps = claim(pe, ("v", t))
                for k in range(KC):
                    mm(ps[:, 0:P], xT[:, k, t * P:(t + 1) * P], wkv[:, k, 3 * P:4 * P], start=(k == 0), stop=(k == KC - 1))
                for k in range(KC):
                    ins = mm(ps[:, P:P + 152], xT[:, k, t * P:(t + 1) * P], wkw[:, k, P:280], start=(k == 0), stop=(k == KC - 1))
                filled(ins, ("v", t))
            signal_release("kv", ("v", TT - 1))
            release(pe.nop(), "kw")

            wait_xT(("mem",))
            for j in range(4):
                wkey = f"mk{j // 2}"
                if j % 2 == 0:
                    wait_loaded(pe, wkey)
                ps = claim(pe, ("mk", j))
                for c in range(2):
                    ins = by_weight(None, wkey, ((2 * j + c) % 4) * P, memT, ps[:, c * S:(c + 1) * S], 512)
                filled(ins, ("mk", j))
                if j % 2:
                    signal_release(wkey, ("mk", j))

            for b in range(2):
                wait_drained(pe, ("z", b))
            ps = claim(pe, ("ch",))
            for b in range(2):
                wait_loaded(pe, f"c{b}")
                w = slot(f"c{b}").rearrange("p (j n) -> p j n", j=16)
                for h in range(2):
                    o = (2 * b + h) * 32
                    for j in range(16):
                        ins = mm(ps[:, o:o + 2 * NCMP], w[:, j, h * P:(h + 1) * P],
                                 blocks[:, b, j, :, :].rearrange("p g n -> p (g n)"), start=(j == 0), stop=(j == 15))
            filled(ins, ("ch",))
            signal_release("c0", ("ch",))
            release(pe.nop(), "c1")

            for h in range(2):
                wkey = f"mv{h}"
                wait_loaded(pe, wkey)
                w = slot(wkey).rearrange("p (k n) -> p k n", k=KC)
                for t in range(TT):
                    ps = claim(pe, ("mv", t, h))
                    for k in range(KC):
                        ins = mm(ps[:, :], memT[:, k, t * P:(t + 1) * P], w[:, k, :], start=(k == 0), stop=(k == KC - 1))
                    filled(ins, ("mv", t, h))
                signal_release(wkey, ("mv", TT - 1, h))

            pe.wait_ge(gelu_out, 1)
            pe.wait_ge(small_loaded, 16 * 12)
            ps = claim(pe, ("c2",))
            for g in range(2):
                for h in range(2):
                    for r in range(2):
                        mm(ps[r * HD:(r + 1) * HD, g * 16:g * 16 + NCMP], w2c[:, 0, h, :],
                           ghid[:, h, g * NCMP:(g + 1) * NCMP], start=(h == 0), stop=(h == 1))
            for g in range(2):
                for h in range(2):
                    ins = mm(ps[0:NCMP, 64 + g * HD:64 + (g + 1) * HD], ghid[:, 2 + h, g * NCMP:(g + 1) * NCMP],
                             w2c[:, 1, h, :], start=(h == 0), stop=(h == 1))
            filled(ins, ("c2",))

            pe.wait_ge(consts_ready, 2)
            ps = claim(pe, ("cmean",))
            for c in range(CC):
                pe.wait_ge(conv_ready, c + 1)
                ins = mm(ps[:, 0:S], onesc[:, :], oT[:, c, :], start=(c == 0), stop=(c == CC - 1))
            filled(ins, ("cmean",))

            for j in range(2):
                wait_drained(pe, ("q", j))
            wait_drained(pe, ("c2",))
            for r in range(2):
                ps = claim(pe, ("sc", r))
                rr = slice(r * HD, (r + 1) * HD)
                for t in range(TT):
                    for c in range(CC):
                        ins = mm(ps[:, (t * CC + c) * 16:(t * CC + c) * 16 + NCMP], qT[rr, c, t * P:(t + 1) * P],
                                 k_cmpT[rr, c // 2, 0:NCMP], start=True, stop=True)
                filled(ins, ("sc", r))
            for g in range(2):
                wait_drained(pe, ("k", g))

            def scores(h):
                c, r = h // 2, h % 2
                rr = slice(r * HD, (r + 1) * HD)
                kk = kT[rr, c // 2, :].rearrange("p (b k) -> p b k", b=2)
                for t in range(TT):
                    n = (t + 1) * P
                    ps = claim(pe, ("s", h, t))
                    ins = mm(ps[:, 0:2 * n], qT[rr, c, t * P:(t + 1) * P], kk[:, :, 0:n], start=True, stop=True)
                    filled(ins, ("s", h, t))

            def attend(h):
                c, r = h // 2, h % 2
                g = c // 2
                pT = claim(pe, ("pT", h, 0))
                pU = claim(pe, ("pT", h, 1))
                pe.wait_ge(prob_ready, 2 * h + 1)
                for b in range(2):
                    nc.tensor.transpose(pT[:, b * P:(b + 1) * P], prob[:, h % 2, 0, b * P:(b + 1) * P], ident[:, :])
                for t in range(TT):
                    ins = nc.tensor.transpose(pT[0:16, (2 + t) * P:(3 + t) * P], pc[:, t, h, :], ident[:, :])
                filled(ins, ("pT", h, 0))
                pe.wait_ge(prob_ready, 2 * h + 2)
                for b in range(2):
                    for kt in range(2):
                        ins = nc.tensor.transpose(pU[:, (2 * b + kt) * P:(2 * b + kt + 1) * P],
                                                  prob[:, h % 2, 1, b * S + kt * P:b * S + (kt + 1) * P], ident[:, :])
                filled(ins, ("pT", h, 1))

            def weigh(h):
                c, r = h // 2, h % 2
                g = c // 2
                ps = claim(pe, ("o", c)) if r == 0 else banks[bank_of[("o", c)][0]]
                po = ps[r * HD:(r + 1) * HD, 0:S]
                wait_drained(pe, ("pT", h, 0))
                wait_drained(pe, ("pT", h, 1))
                for b in range(2):
                    mm(po, v_sb[:, 0, b, g * HD:(g + 1) * HD], probT[:, h % 2, b, 0, :], start=(b == 0), stop=False)
                    mm(po[:, P:S], v_sb[:, 1, b, g * HD:(g + 1) * HD], probT[:, h % 2, b, 1, P:S], start=False, stop=False)
                ins = mm(po, v_cmp[0:NCMP, g, :], pcT[0:NCMP, h % 2, :], start=False, stop=True)
                if r == 1:
                    filled(ins, ("o", c))

            pe.wait_ge(cprob, 1)
            for t in range(TT):
                wait_drained(pe, ("v", t))
            scores(0)
            for h in range(HEADS):
                if h + 1 < HEADS:
                    scores(h + 1)
                attend(h)
                if h > 0:
                    weigh(h - 1)
                if h == 2:
                    ps = claim(pe, ("cvar",))
                    for c in range(CC):
                        pe.wait_ge(sq_ready, c + 1)
                        ins = mm(ps[:, 0:S], onesc[:, :], aT[:, c, PAD:PAD + S], start=(c == 0), stop=(c == CC - 1))
                    filled(ins, ("cvar",))
            weigh(HEADS - 1)
            pe.wait_ge(a_out, CC)
            for c in range(CC):
                wait_drained(pe, ("o", c))

            for L in range(DEPTH):
                if L == 1:
                    wait_xT(("n", 2))
                    for h in range(2):
                        for part in "chb":
                            wait_loaded(pe, f"od_{part}{h}")
                        for c in range(4):
                            ps = claim(pe, ("odc", 4 * h + c))
                            by_weight(None, f"od_c{h}", c * P, xT, ps[:, 0:S], 512)
                            filled(by_weight(None, f"od_h{h}", c * P, xT, ps[:, S:2 * S], 512), ("odc", 4 * h + c))
                            ps = claim(pe, ("odb", 4 * h + c))
                            filled(by_weight(None, f"od_b{h}", c * P, xT, ps[:, 0:S], 512), ("odb", 4 * h + c))
                        signal_release(f"od_c{h}", ("odb", 4 * h + 3))
                        release(pe.nop(), f"od_h{h}")
                        release(pe.nop(), f"od_b{h}")
                    for c in range(KC):
                        wait_drained(pe, ("odb", c))
                out_projection(f"wo_mix{L}", 3 * L)

                transposed(("n", 3 * L), x)
                wait_xT(("n", 3 * L))
                for j in range(4):
                    wkey = f"xq{L}{j // 2}"
                    if j % 2 == 0:
                        wait_loaded(pe, wkey)
                    ps = claim(pe, ("xq", L, j))
                    for c in range(2):
                        ins = by_weight(None, wkey, ((2 * j + c) % 4) * P, xT, ps[:, c * S:(c + 1) * S], 512)
                    filled(ins, ("xq", L, j))
                    if j % 2:
                        signal_release(wkey, ("xq", L, j))
                if L == 0:
                    for j in range(4):
                        wait_drained(pe, ("mk", j))
                        wait_drained(pe, ("mv", j % 2, j // 2))

                def xscores(h):
                    wait_drained(pe, ("xq", L, h))
                    ps = claim(pe, ("xs", L, h))
                    for t in range(TT):
                        for c in range(2):
                            ins = mm(ps[:, t * S:(t + 1) * S], qxT[:, 2 * h + c, t * P:(t + 1) * P],
                                     mem_kT[:, 2 * h + c, :], start=(c == 0), stop=(c == 1))
                    filled(ins, ("xs", L, h))

                def xattend(h):
                    pe.wait_ge(prob_ready, 2 * HEADS + L * XH + h + 1)
                    ps = claim(pe, ("xp", L, h))
                    for m in range(2):
                        for t in range(TT):
                            ins = nc.tensor.transpose(ps[:, (2 * m + t) * P:(2 * m + t + 1) * P],
                                                      prob[:, h % 2, t, m * P:(m + 1) * P], ident[:, :])
                    filled(ins, ("xp", L, h))

                def xweigh(h):
                    wait_drained(pe, ("xp", L, h))
                    ps = claim(pe, ("xo", L, h))
                    for c in range(2):
                        for m in range(2):
                            ins = mm(ps[:, c * S:(c + 1) * S], mem_v[:, m, (2 * h + c) * P:(2 * h + c + 1) * P],
                                     probT[:, h % 2, 0, m, :], start=(m == 0), stop=(m == 1))
                    filled(ins, ("xo", L, h))

                xscores(0)
                for h in range(XH):
                    if h + 1 < XH:
                        xscores(h + 1)
                    xattend(h)
                    if h > 0:
                        xweigh(h - 1)
                xweigh(XH - 1)
                for h in range(XH):
                    wait_drained(pe, ("xo", L, h))
                out_projection(f"xo{L}", 3 * L + 1)

                transposed(("n", 3 * L + 1), x)
                wait_xT(("n", 3 * L + 1))
                ps = claim(pe, ("lg", L))
                for t in range(TT):
                    for k in range(KC):
                        ins = mm(ps[:, t * 64:t * 64 + NG + NE], xT[:, k, t * P:(t + 1) * P], wr[:, L, k, :],
                                 start=(k == 0), stop=(k == KC - 1))
                filled(ins, ("lg", L))
                pe.wait_ge(mask_ready, L + 1)
                ps = claim(pe, ("pos", L))
                mm(ps[:, 0:NE], tri[:, :], mask[:, 0, :], start=True, stop=True)
                mm(ps[:, NE:2 * NE], tri[:, :], mask[:, 1, :], start=True, stop=False)
                mm(ps[:, NE:2 * NE], ones[:, :], mask[:, 0, :], start=False, stop=True)
                mm(ps[:, 64:64 + NE], ones[:, :], mask[:, 0, :], start=True, stop=False)
                filled(mm(ps[:, 64:64 + NE], ones[:, :], mask[:, 1, :], start=False, stop=True), ("pos", L))

                acc = []
                for t in range(TT):
                    for h in range(2):
                        acc.append(claim(pe, ("f", 3 * L + 2, t, h), bank=2 * t + h))
                for b in range(4, 8):
                    pe.wait_ge(bank_drained[b], fills[b])
                rotation[0] = 4
                b1, b3 = banks[4:6]
                bY = banks[6:8]
                for a in acc:
                    mm(a[:, :], zero16[:, 0:P], zero16[:, :], start=True, stop=False, skip_group_check=True)

                def gather(fam, d):
                    for k in range(KC):
                        for t in range(TT):
                            src = x[:, t, :].rearrange("p (q k) -> p k q", k=KC)[:, k, :]
                            ins = mm(bY[k // 4][:, (k % 4) * P:(k % 4 + 1) * P], src, d[:, t, :, :].rearrange("p e s -> p (e s)"),
                                     start=(t == 0), stop=(t == TT - 1))
                        if k % 4 == 3:
                            ins.then_inc(fam.gather_done, 1)

                def hidden(fam, m, xg):
                    for k in range(KC):
                        for j in range(2):
                            w = ring[:, 2 * m + j, :].rearrange("p (k n) -> p k n", k=KC)
                            ins = mm((b1, b3)[m][j * CAP:(j + 1) * CAP, :], xg[:, k, j * CAP:(j + 1) * CAP], w[:, k, :],
                                     start=(k == 0), stop=(k == KC - 1))
                    ins.then_inc((fam.w1_used, fam.hid_done)[m], 1)

                def turn(fam, dg):
                    for c in range(4):
                        ins = nc.tensor.transpose(b1[:, c * P:(c + 1) * P], hid[:, :].rearrange("p (q c) -> p c q", c=4)[:, c, :], ident[:, :])
                    ins.then_inc(fam.hidT_done, 1)
                    for t in range(TT):
                        ins = nc.tensor.transpose(b3[:, t * P:(t + 1) * P], dg[:, t, :, :].rearrange("p e s -> p (e s)"), ident[:, :])
                    ins.then_inc(fam.comb_done, 1)

                def results(fam):
                    for c in range(4):
                        for h in range(2):
                            for j in range(2):
                                w = ring[:, 4 + j, :].rearrange("p (c n) -> p c n", c=4)
                                ins = mm(bY[h][j * CAP:(j + 1) * CAP, :], hidT[:, c, j * CAP:(j + 1) * CAP],
                                         w[:, c, h * 512:(h + 1) * 512], start=(c == 0), stop=(c == 3))
                    ins.then_inc(fam.y_done, 1)

                def scatter(fam, cb, yy):
                    for t in range(TT):
                        for h in range(2):
                            ins = mm(acc[2 * t + h][:, :], cb[:, t * P:(t + 1) * P], yy[:, h * 512:(h + 1) * 512],
                                     start=False, stop=False, skip_group_check=True)
                    ins.then_inc(fam.scattered, 1)

                g0 = L * (PAIRS + 1)
                for t in range(TT):
                    pe.wait_ge(x_ready, 2 * (3 * L + 1) + t + 1)
                pe.wait_ge(main.disp_built, g0 + 1)
                gather(main, disp)
                pe.wait_ge(rounds_ready, L + 1)
                with pe.Fori(0, PAIRS) as i:
                    n1 = i + (L * PAIRS + 1)
                    pe.wait_ge(main.gathered, i * 2 + 2 * (g0 + 1))
                    for m in range(2):
                        for j in range(2):
                            s = 2 * m + j
                            pe.wait_ge(loaded[s], (i + (moe_base[L][s] + 1)) * 16)
                        if m == 1:
                            pe.wait_ge(main.comb_ready, i + (g0 + 1))
                        hidden(main, m, xgT)
                    pe.wait_ge(main.y_ready, i + (g0 + 1))
                    pe.wait_ge(main.disp_built, i + (g0 + 2))
                    gather(main, disp)
                    pe.wait_ge(main.hidden_ready, n1)
                    pe.wait_ge(main.disp_gated, i + (g0 + 1))
                    turn(main, dispg)
                    scatter(main, comb, y)
                    for s in (4, 5):
                        pe.wait_ge(loaded[s], (i + (moe_base[L][s] + 1)) * 16)
                    pe.wait_ge(main.hidT_ready, n1)
                    pe.wait_ge(main.gathered, i * 2 + 2 * (g0 + 2))
                    results(main)
                    n, before = load_rounds(pe, i)
                    with pe.Fori(0, ROUNDS - 1) as q:
                        with pe.If(n > q):
                            fam = over[L]
                            k1 = before + q + 1
                            pe.wait_ge(main.y_ready, i + (g0 + 2))
                            pe.wait_ge(main.comb_ready, i + (g0 + 2))
                            pe.wait_ge(fam.disp_built, k1)
                            gather(fam, more_disp)
                            pe.wait_ge(fam.gathered, k1 * 2)
                            hidden(fam, 0, more_xgT)
                            hidden(fam, 1, more_xgT)
                            pe.wait_ge(fam.hidden_ready, k1)
                            pe.wait_ge(fam.disp_gated, k1)
                            turn(fam, more_dispg)
                            pe.wait_ge(fam.hidT_ready, k1)
                            results(fam)
                            pe.wait_ge(fam.y_ready, k1)
                            pe.wait_ge(fam.comb_ready, k1)
                            scatter(fam, more_comb, more_y)
                pe.wait_ge(main.y_ready, g0 + PAIRS + 1)
                pe.wait_ge(main.comb_ready, g0 + PAIRS + 1)
                scatter(main, comb, y)
                for t in range(TT):
                    for h in range(2):
                        key = ("f", 3 * L + 2, t, h)
                        filled(mm(acc[2 * t + h][:, :], zero16[:, 0:P], zero16[:, :], start=False, stop=True,
                                  skip_group_check=True), key)
                if L + 1 < DEPTH:
                    transposed(("n", 3 * L + 2), x)

        def norm_dve(st, v, i):
            for t in range(TT):
                for h in range(2):
                    key = ("f", i, t, h)
                    ps = wait_filled(v, key)
                    xx = x[:, t, h * 512:(h + 1) * 512]
                    drained(nc.vector.scalar_tensor_tensor(out=xx, in0=xx, scalar=ALPHA, in1=ps[:, :], op0=ALU.mult, op1=ALU.add), key)
                for h in range(2):
                    wait_drained(v, ("f", i, t, h))
                    st.mark(nc.vector.bn_stats(out=bn[:, t, h, :], in_=x[:, t, h * 512:(h + 1) * 512]))
                st.wait()
                nc.vector.bn_aggr(out=mv[:, t, :], in_=bn[:, t, :, :].rearrange("p a b -> p (a b)")).then_inc(ln_stats, 1)
            for t in range(TT):
                v.wait_ge(ln_rstd, 2 * i + t + 1)
                nc.vector.tensor_scalar(x[:, t, :], x[:, t, :], mv[:, t, 0:1], rstd[:, t, :], ALU.subtract, ALU.mult).then_inc(n_ready, 1)
            if i == 0:
                v.wait_ge(small_loaded, 16 * 12)
            if i < LN_COUNT - 1:
                for t in range(TT):
                    ps = wait_filled(v, (("n", i), t, 1))
                    pv = ps[:, :].rearrange("p (k s) -> p k s", k=4)
                    o = xT[:, 4:8, t * P:(t + 1) * P]
                    st.do(nc.vector.tensor_tensor(o, pv, lngT[:, i, 0, 4:8].unsqueeze(2).to_broadcast([P, 4, P]), ALU.mult))
                    drained(nc.vector.tensor_tensor(o, o, lngT[:, i, 1, 4:8].unsqueeze(2).to_broadcast([P, 4, P]), ALU.add), (("n", i), t, 1))
            v.wait_ge(gb_loaded, 32 * (i + 1))
            for t in range(TT):
                if i < LN_COUNT - 1:
                    wait_filled(v, (("n", i), t, 0))
                else:
                    v.wait_ge(n_ready, 2 * i + t + 1)
                st.mark(nc.vector.tensor_tensor(x[:, t, :], x[:, t, :], gb[:, 0, :], ALU.mult))
            a = st.n
            for t in range(TT):
                st.wait(a - 1 + t)
                nc.vector.tensor_tensor(x[:, t, :], x[:, t, :], gb[:, 1, :], ALU.add).then_inc(x_ready, 1)

        def norm_act(a, i):
            for t in range(TT):
                ps = wait_filled(a, (("n", i), t, 0))
                for k in range(4):
                    ins = nc.scalar.activation(xT[:, k, t * P:(t + 1) * P], ps[:, k * P:(k + 1) * P], ACT.Identity,
                                               scale=lngT[:, i, 0, k:k + 1], bias=lngT[:, i, 1, k:k + 1])
                drained(ins, (("n", i), t, 0))

        @block.vector
        def _(v):
            st = Steps(v, dve_step)
            tt, ts, stt, cp = nc.vector.tensor_tensor, nc.vector.tensor_scalar, nc.vector.scalar_tensor_tensor, nc.vector.tensor_copy

            nc.vector.memset(aT[:, :, 0:PAD], 0.0)
            nc.vector.memset(g8[:, :, :], NEG)
            nc.vector.memset(place[:, :, NE:NE + 2], -1.0)
            nc.vector.memset(gate[:, :, NE:NE + 2], 0.0)
            st.do(nc.vector.memset(pc[:, :, :, :], 0.0))
            zeros_set = st.n
            for t in range(TT):
                for h in range(2):
                    if h:
                        ps = wait_filled(v, (("x",), t, h))
                        drained(cp(xT[:, 4 * h:4 * h + 4, t * P:(t + 1) * P], ps[:, :].rearrange("p (k s) -> p k s", k=4)), (("x",), t, h))
            ps = wait_filled(v, ("cols",))
            ts(cw[:, 0:TAPS * CC], ps[:, 0:TAPS * CC], 0.5, None, ALU.mult)
            drained(cp(cols[:, :], ps[:, P:P + C_ALL]), ("cols",))
            wait_drained(v, ("cols",))
            for c in range(CC):
                v.wait_ge(sig_ready, c + 1)
                ps = banks[bank_of[("a", c)][0]]
                drained(stt(out=aT[:, c, PAD:PAD + S], in0=scr[:, c % 2, :], scalar=1.0, in1=ps[:, 0:S], op0=ALU.add, op1=ALU.mult), ("a", c))
            for t in range(TT):
                ps = wait_filled(v, (("mem",), t, 1))
                drained(cp(memT[:, 4:8, t * P:(t + 1) * P], ps[:, :].rearrange("p (k s) -> p k s", k=4)), (("mem",), t, 1))
            for c in range(CC):
                wait_drained(v, ("a", c))
            def compress_input(b):
                ps = wait_filled(v, ("z", b))
                tok = ps[:, :].rearrange("p (g a r two) -> p r g a two", g=2, a=16, two=2)[:, :, :, :, 0]
                for jh in range(2):
                    pe_ = cols[:, (C_PK, C_PV)[b] + 8 * jh:(C_PK, C_PV)[b] + 8 * jh + 8]
                    for g in range(2):
                        ins = tt(blocks[:, b, 8 * jh:8 * jh + 8, g, :], tok[:, :, g, jh:jh + NCMP],
                                 pe_.unsqueeze(2).to_broadcast([P, 8, NCMP]), ALU.add)
                drained(ins, ("z", b))

            base = st.n
            for k in range(TAPS):
                for c in range(CC):
                    w = cw[:, k * CC + c:k * CC + c + 1]
                    src = aT[:, c, k:k + S]
                    if k == 0:
                        st.mark(ts(oT[:, c, :], src, w, cols[:, C_CB + c:C_CB + c + 1], ALU.mult, ALU.add))
                        continue
                    st.wait(base + (k - 1) * CC + c + 1)
                    ins = stt(out=oT[:, c, :], in0=src, scalar=w, in1=oT[:, c, :], op0=ALU.mult, op1=ALU.add)
                    if k < TAPS - 1:
                        st.mark(ins)
                    else:
                        ins.then_inc(conv_ready, 1)
            compress_input(0)
            compress_input(1)
            ps = wait_filled(v, ("ch",))
            hv = ps[:, 0:P].rearrange("p (a n) -> p a n", n=32)[:, :, 0:2 * NCMP]
            hh, gt = ghid[:, :, 0:2 * NCMP], gtmp[:, :, 0:2 * NCMP]
            st.do(cp(hh, hv))
            st.do(tt(gt, hh, hh, ALU.mult))
            st.do(ts(gt, gt, GELU_A, 1.0, ALU.mult, ALU.add))
            drained(tt(gt, gt, hh, ALU.mult), ("ch",))
            v.wait_ge(gelu_tanh, 1)
            stt(out=hh, in0=gt, scalar=1.0, in1=hh, op0=ALU.add, op1=ALU.mult).then_inc(gelu_out, 1)
            wait_drained(v, ("v", 0))
            wait_drained(v, ("v", 1))
            st.do(ts(gates[:, :, :], gates[:, :, :], 0.5, 0.5, ALU.mult, ALU.add))

            ps = wait_filled(v, ("cmean",))
            for c in range(CC):
                ins = tt(oT[:, c, :], oT[:, c, :], ps[:, 0:S], ALU.subtract)
                if c < CC - 1:
                    st.mark(ins)
            drained(ins, ("cmean",))
            wait_drained(v, ("cmean",))
            for c in range(CC):
                tt(aT[:, c, PAD:PAD + S], oT[:, c, :], oT[:, c, :], ALU.mult).then_inc(sq_ready, 1)

            st.wait(zeros_set)
            v.wait_ge(consts_ready, 2)
            gv = gates[:, :, :].rearrange("p t (h b) -> p t h b", b=3)
            for r in range(2):
                ps = wait_filled(v, ("sc", r))
                for t in range(TT):
                    sv = ps[:, t * 64:(t + 1) * 64].rearrange("p (c n) -> p c n", n=16)[:, :, 0:NCMP]
                    pv = pc[:, t, :, :].rearrange("p (c r) n -> p r c n", r=2)[:, r, :, 0:NCMP]
                    ins = tt(pv, sv, cbias[:, t, 0:NCMP].unsqueeze(1).to_broadcast([P, CC, NCMP]), ALU.add)
                    if t == 0:
                        st.mark(ins)
                drained(ins, ("sc", r))
                wait_drained(v, ("sc", r))
            pcv = pc[:, :, :, 0:NCMP]
            mx = stat[:, 0:16].rearrange("p (t h) -> p t h", t=TT)
            sm = stat[:, 16:32].rearrange("p (t h) -> p t h", t=TT)
            st.do(nc.vector.tensor_reduce(mx, pcv, AX, ALU.max))
            for t in range(TT):
                ins = tt(pc[:, t, :, 0:NCMP], pc[:, t, :, 0:NCMP], mx[:, t, :].unsqueeze(2).to_broadcast([P, HEADS, NCMP]), ALU.subtract)
                if t == 0:
                    st.mark(ins)
            ins.then_inc(cmax, 1)
            v.wait_ge(cexp, 1)
            st.do(nc.vector.tensor_reduce(sm, pcv, AX, ALU.add))
            st.do(nc.vector.reciprocal(sm, sm))
            st.do(tt(sm, sm, gv[:, :, :, 0], ALU.mult))
            for t in range(TT):
                w = pc[:, t, :, 0:NCMP]
                st.do(tt(w, w, sm[:, t, :].unsqueeze(2).to_broadcast([P, HEADS, NCMP]), ALU.mult))
                ins = tt(w, w, cmask[:, t, 0:NCMP].unsqueeze(1).to_broadcast([P, HEADS, NCMP]), ALU.mult)
                if t == 0:
                    st.mark(ins)
            ins.then_inc(cprob, 1)

            def soft_in(h, t):
                n = (t + 1) * P
                ps = wait_filled(v, ("s", h, t))
                sv = ps[:, 0:2 * n].rearrange("p (b k) -> p b k", b=2)
                dg = sv[:, :, t * P:(t + 1) * P]
                st.do(tt(dg, dg, causal[:, :].unsqueeze(1).to_broadcast([P, 2, P]), ALU.add))
                o = 32 + 8 * (h % 2) + 4 * t
                nc.vector.tensor_reduce(stat[:, o:o + 2], sv, AX, ALU.max, negate=True).then_inc(neg_max, 1)

            def soft_out(h, t):
                n = (t + 1) * P
                o = 32 + 8 * (h % 2) + 4 * t
                wait_drained(v, ("s", h, t))
                s2 = stat[:, o + 2:o + 4]
                st.do(nc.vector.reciprocal(s2, s2))
                st.do(tt(s2, s2, gv[:, t, h, 1:3], ALU.mult))
                pv = prob[:, h % 2, t, 0:2 * n].rearrange("p (b k) -> p b k", b=2)
                tt(pv, pv, s2.unsqueeze(2).to_broadcast([P, 2, n]), ALU.mult).then_inc(prob_ready, 1)

            def evac_pU(h):
                ps = wait_filled(v, ("pT", h, 1))
                drained(cp(probT[:, h % 2, :, :, P:S], ps[:, :].rearrange("p (b k q) -> p b k q", b=2, k=2)), ("pT", h, 1))

            soft_in(0, 0)
            soft_in(0, 1)
            for h in range(HEADS):
                soft_out(h, 0)
                soft_out(h, 1)
                if h + 1 < HEADS:
                    soft_in(h + 1, 0)
                    soft_in(h + 1, 1)
                evac_pU(h)
                if h == 4:
                    v.wait_ge(stat_ready, 1)
                    for c in range(CC):
                        st.mark(tt(oT[:, c, :], oT[:, c, :], scr[:, 1, :], ALU.mult))
                    st.wait()
                    for c in range(CC):
                        ts(oT[:, c, :], oT[:, c, :], cols[:, C_CG + c:C_CG + c + 1], cols[:, C_CN + c:C_CN + c + 1],
                           ALU.mult, ALU.add).then_inc(convn_ready, 1)
                if h == 5:
                    for c in range(CC):
                        v.wait_ge(convt_ready, c + 1)
                        st.mark(stt(out=oT[:, c, :], in0=aT[:, c, PAD:PAD + S], scalar=1.0, in1=oT[:, c, :], op0=ALU.add, op1=ALU.mult))
                    st.wait()
                    for c in range(CC):
                        ts(oT[:, c, :], oT[:, c, :], 0.5, None, ALU.mult).then_inc(a_out, 1)

            for L in range(DEPTH):
                if L == 1:
                    for c in range(KC):
                        pch = wait_filled(v, ("odc", c))
                        v.wait_ge(od_c, c + 1)
                        ub = aT[:, c % 2, PAD - 2:PAD + S]
                        st.do(tt(aT[:, c % 2, PAD:PAD + S], scr[:, c % 2, :], pch[:, S:2 * S], ALU.mult))
                        w = [cols[:, C_OD + 8 * k + c:C_OD + 8 * k + c + 1] for k in range(3)]
                        drained(ts(u[:, :], ub[:, 2:2 + S], w[2], None, ALU.mult), ("odc", c))
                        wait_drained(v, ("odc", c))
                        for k in (1, 0):
                            st.do(stt(out=u[:, :], in0=ub[:, k:k + S], scalar=w[k], in1=u[:, :], op0=ALU.mult, op1=ALU.add))
                        ps = wait_filled(v, ("odb", c))
                        drained(tt(oT[:, c, :], u[:, :], ps[:, 0:S], ALU.mult), ("odb", c))
                norm_dve(st, v, 3 * L)

                def x_in(h):
                    ps = wait_filled(v, ("xs", L, h))
                    o = 32 + 8 * (h % 2)
                    nc.vector.tensor_reduce(stat[:, o:o + 2], ps[:, :].rearrange("p (t k) -> p t k", t=2), AX, ALU.max, negate=True).then_inc(neg_max, 1)

                def x_out(h):
                    o = 32 + 8 * (h % 2)
                    wait_drained(v, ("xs", L, h))
                    s2 = stat[:, o + 2:o + 4]
                    st.do(nc.vector.reciprocal(s2, s2))
                    pv = prob[:, h % 2, :, 0:S]
                    tt(pv, pv, s2.unsqueeze(2).to_broadcast([P, 2, S]), ALU.mult).then_inc(prob_ready, 1)

                x_in(0)
                for h in range(XH):
                    x_out(h)
                    if h + 1 < XH:
                        x_in(h + 1)
                    ps = wait_filled(v, ("xp", L, h))
                    drained(cp(probT[:, h % 2, 0, :, :], ps[:, :].rearrange("p (m s) -> p m s", m=2)), ("xp", L, h))
                norm_dve(st, v, 3 * L + 1)

                ps = wait_filled(v, ("lg", L))
                v.wait_ge(bias_loaded, 32)
                drained(tt(lg[:, :, :], ps[:, 0:128].rearrange("p (t n) -> p t n", t=TT)[:, :, 0:NG + NE],
                           rbias[:, L, :].unsqueeze(1).to_broadcast([P, TT, NG + NE]), ALU.add), ("lg", L))
                wait_drained(v, ("lg", L))
                st.do(cp(g8[:, :, 0:NG], lg[:, :, 0:NG]))
                for t in range(TT):
                    st.mark(nc.vector.max(top[:, t, 0, :], g8[:, t, :]))
                st.wait()
                for t in range(TT):
                    st.mark(nc.vector.max_index(topi[:, t, 0, :], top[:, t, 0, :], g8[:, t, :]))
                st.mark(ts(rs[:, 0, :], top[:, :, 0, 0], -1.0, None, ALU.mult))
                st.wait()
                cp(topf[:, :, 0, :], topi[:, :, 0, :]).then_inc(gexp_in, 1)
                v.wait_ge(gexp_in, L + 1)
                st.do(tt(ohg[:, :, :], iota[:, 0:NG].unsqueeze(1).to_broadcast([P, TT, NG]),
                         topf[:, :, 0, 0:1].to_broadcast([P, TT, NG]), ALU.is_equal))
                ev = lg[:, :, NG:NG + NE].rearrange("p t (g e) -> p t g e", g=NG)
                for t in range(TT):
                    st.mark(tt(etmp[:, t, :, :], ev[:, t, :, :], ohg[:, t, :].unsqueeze(2).to_broadcast([P, NG, EPG]), ALU.mult))
                st.wait()
                for t in range(TT):
                    st.mark(nc.vector.tensor_reduce(esel[:, t, :], etmp[:, t, :, :].rearrange("p g e -> p e g"), AX, ALU.add))
                st.wait()
                for t in range(TT):
                    st.mark(nc.vector.max(top[:, t, 1, :], esel[:, t, :]))
                st.wait()
                for t in range(TT):
                    st.mark(nc.vector.max_index(topi[:, t, 1, :], top[:, t, 1, :], esel[:, t, :]))
                st.wait()
                tt(rs[:, 2, :], top[:, :, 1, 1], top[:, :, 1, 0], ALU.subtract).then_inc(eexp_in, 1)
                st.do(cp(topf[:, :, 1, :], topi[:, :, 1, :]))
                for m in range(2):
                    st.mark(tt(e01[:, m, :, :], iota[:, 0:EPG].unsqueeze(1).to_broadcast([P, TT, EPG]),
                               topf[:, :, 1, m:m + 1].to_broadcast([P, TT, EPG]), ALU.is_equal))
                st.wait()
                st.do(tt(esel[:, :, :], e01[:, 0, :, :], e01[:, 1, :, :], ALU.add))
                mk = mask[:, :, :].rearrange("p t (g e) -> p t g e", g=NG)
                for t in range(TT):
                    ins = tt(mk[:, t, :, :], ohg[:, t, :].unsqueeze(2).to_broadcast([P, NG, EPG]),
                             esel[:, t, :].unsqueeze(1).to_broadcast([P, NG, EPG]), ALU.mult)
                    if t == 0:
                        st.mark(ins)
                ins.then_inc(mask_ready, 1)
                v.wait_ge(gexp, L + 1)
                v.wait_ge(eexp, L + 1)
                st.do(ts(rs[:, 4, :], rs[:, 3, :], 1.0, None, ALU.add))
                st.do(tt(rs[:, 4, :], rs[:, 4, :], rs[:, 1, :], ALU.mult))
                st.do(nc.vector.reciprocal(rs[:, 4, :], rs[:, 4, :]))
                st.do(tt(rs[:, 5, :], rs[:, 4, :], rs[:, 3, :], ALU.mult))
                for m in range(2):
                    st.mark(tt(e01[:, m, :, :], e01[:, m, :, :], rs[:, 4 + m, :].unsqueeze(2).to_broadcast([P, TT, EPG]), ALU.mult))
                st.wait()
                v.wait_ge(mask_ready, L + 1)
                st.do(tt(esel[:, :, :], e01[:, 0, :, :], e01[:, 1, :, :], ALU.add))
                for t in range(TT):
                    st.mark(tt(gate[:, t, 0:NE].rearrange("p (g e) -> p g e", g=NG), ohg[:, t, :].unsqueeze(2).to_broadcast([P, NG, EPG]),
                               esel[:, t, :].unsqueeze(1).to_broadcast([P, NG, EPG]), ALU.mult))
                ps = wait_filled(v, ("pos", L))
                pv = ps[:, 0:2 * NE].rearrange("p (t e) -> p t e", t=TT)
                st.do(stt(out=place[:, :, 0:NE], in0=pv, scalar=1.0, in1=mask[:, :, :], op0=ALU.add, op1=ALU.mult))
                st.do(ts(place[:, :, 0:NE], place[:, :, 0:NE], -1.0, None, ALU.add))
                st.do(nc.vector.tensor_reduce(counts[:, 0, :], ps[:, 64:64 + NE].rearrange("p (i j) -> p i j", j=2), AX, ALU.max))
                drained(ts(counts[:, 1, :], counts[:, 0, :], float(CAP), None, ALU.is_gt), ("pos", L))
                wait_drained(v, ("pos", L))
                for r_ in (2, 3):
                    st.do(stt(out=counts[:, 1, :], in0=counts[:, 0, :], scalar=float(r_ * CAP), in1=counts[:, 1, :], op0=ALU.is_gt, op1=ALU.add))
                st.do(nc.vector.tensor_copy(rounds[:, :, 0], counts[:, 1, :]))
                a_, b_ = 1, 2
                for step in (1, 2, 4, 8):
                    st.mark(cp(counts[:, b_, 0:step], counts[:, a_, 0:step]))
                    st.do(tt(counts[:, b_, step:PAIRS], counts[:, a_, step:PAIRS], counts[:, a_, 0:PAIRS - step], ALU.add))
                    a_, b_ = b_, (3 if a_ == 1 else a_)
                st.mark(nc.vector.memset(rounds[:, 0, 1:2], 0))
                cp(rounds[:, 1:PAIRS, 1], counts[:, a_, 0:PAIRS - 1]).then_inc(rounds_ready, 1)

                def place_of(t_, pair):
                    return t_[:, :, bass.ds(pair * 2, 2)] if not isinstance(pair, int) else t_[:, :, 2 * pair:2 * pair + 2]

                def build(fam, d, places):
                    return tt(d, iota[:, :].unsqueeze(1).unsqueeze(1).to_broadcast([P, TT, 2, CAP]),
                              places.unsqueeze(3).to_broadcast([P, TT, 2, CAP]), ALU.is_equal).then_inc(fam.disp_built, 1)

                def weight(fam, d, dg, pair):
                    tt(dg, d, place_of(gate, pair).unsqueeze(3).to_broadcast([P, TT, 2, CAP]), ALU.mult).then_inc(fam.disp_gated, 1)

                def take(fam, xg, h):
                    cp(xg[:, 4 * h:4 * h + 4, :], banks[6 + h][:, :].rearrange("p (k s) -> p k s", k=4)).then_inc(fam.gathered, 1)

                def silu_in(fam):
                    stt(out=u512, in0=th, scalar=1.0, in1=banks[4][:, :], op0=ALU.add, op1=ALU.mult).then_inc(fam.glu_done, 1)

                def glu_out(fam):
                    stt(out=hid, in0=u512, scalar=0.5, in1=banks[5][:, :], op0=ALU.mult, op1=ALU.mult).then_inc(fam.hidden_ready, 1)

                g0 = L * (PAIRS + 1)
                st.wait()
                nc.vector.memset(comb, 0.0).then_inc(main.comb_ready, 1)
                nc.vector.memset(y, 0.0).then_inc(main.y_ready, 1)
                build(main, disp, place_of(place, 0))
                v.wait_ge(main.disp_built, g0 + 1)
                weight(main, disp, dispg, 0)
                for h in range(2):
                    v.wait_ge(main.gather_done, 2 * g0 + h + 1)
                    take(main, xgT, h)
                v.wait_ge(rounds_ready, L + 1)
                with v.Fori(0, PAIRS) as i:
                    n1 = i + (L * PAIRS + 1)
                    v.wait_ge(main.disp_gated, i + (g0 + 1))
                    v.wait_ge(main.gather_done, i * 2 + 2 * (g0 + 1))
                    build(main, disp, place_of(place, i + 1))
                    v.wait_ge(main.tanh_done, n1)
                    silu_in(main)
                    v.wait_ge(main.glu_done, n1)
                    glu_out(main)
                    for h in range(2):
                        v.wait_ge(main.gather_done, i * 2 + (2 * (g0 + 1) + h + 1))
                        take(main, xgT, h)
                    v.wait_ge(main.comb_done, n1)
                    v.wait_ge(main.disp_built, i + (g0 + 2))
                    weight(main, disp, dispg, i + 1)
                    n, before = load_rounds(v, i)
                    with v.Fori(0, ROUNDS - 1) as q:
                        with v.If(n > q):
                            fam = over[L]
                            k1 = before + q + 1
                            v.wait_ge(main.y_done, n1)
                            ts(shifted[:, :, :], place_of(place, i), round_caps[:, bass.ds(q, 1)], None, ALU.subtract).then_inc(shift_done[L], 1)
                            v.wait_ge(shift_done[L], k1)
                            build(fam, more_disp, shifted[:, :, :])
                            for h in range(2):
                                v.wait_ge(fam.gather_done, k1 * 2 - 1 + h)
                                take(fam, more_xgT, h)
                            v.wait_ge(fam.disp_built, k1)
                            weight(fam, more_disp, more_dispg, i)
                            v.wait_ge(fam.disp_gated, k1)
                            v.wait_ge(fam.tanh_done, k1)
                            silu_in(fam)
                            v.wait_ge(fam.glu_done, k1)
                            glu_out(fam)
                norm_dve(st, v, 3 * L + 2)

        @block.scalar
        def _(a):
            st = Steps(a, act_step)
            act, cp = nc.scalar.activation, nc.scalar.copy
            for t in range(TT):
                ps = wait_filled(a, (("x",), t, 0))
                drained(cp(xT[:, 0:4, t * P:(t + 1) * P], ps[:, :].rearrange("p (k s) -> p k s", k=4)), (("x",), t, 0))
            for c in range(CC):
                ps = wait_filled(a, ("a", c))
                if c >= 2:
                    wait_drained(a, ("a", c - 2))
                act(scr[:, c % 2, :], ps[:, S:2 * S], ACT.Tanh, scale=0.5).then_inc(sig_ready, 1)
            for t in range(TT):
                ps = wait_filled(a, (("mem",), t, 0))
                drained(cp(memT[:, 0:4, t * P:(t + 1) * P], ps[:, :].rearrange("p (k s) -> p k s", k=4)), (("mem",), t, 0))
            for j in range(2):
                ps = wait_filled(a, ("q", j))
                drained(nc.scalar.mul(qT[:, 2 * j:2 * j + 2, :], ps[:, :].rearrange("p (c s) -> p c s", c=2), HD ** -0.5), ("q", j))
            for g in range(2):
                ps = wait_filled(a, ("k", g))
                drained(cp(kT[:, g, :], ps[:, :]), ("k", g))
            for t in range(TT):
                ps = wait_filled(a, ("v", t))
                cp(v_sb[:, t, :, :], ps[:, 0:2 * P].rearrange("p (b n) -> p b n", b=2))
                ins = act(gates[:, t, :], ps[:, 2 * P:2 * P + 24], ACT.Tanh, scale=0.5)
                drained(ins, ("v", t))
            for j in range(4):
                ps = wait_filled(a, ("mk", j))
                drained(nc.scalar.mul(mem_kT[:, 2 * j:2 * j + 2, :], ps[:, :].rearrange("p (c s) -> p c s", c=2), (D // XH) ** -0.5), ("mk", j))
            wait_drained(a, ("ch",))
            act(gtmp[:, :, 0:2 * NCMP], gtmp[:, :, 0:2 * NCMP], ACT.Tanh, scale=GELU_B).then_inc(gelu_tanh, 1)
            for h in range(2):
                for t in range(TT):
                    ps = wait_filled(a, ("mv", t, h))
                    drained(cp(mem_v[:, t, h * 512:(h + 1) * 512], ps[:, :]), ("mv", t, h))
            ps = wait_filled(a, ("c2",))
            nc.scalar.mul(k_cmpT[:, :, 0:NCMP], ps[:, 0:32].rearrange("p (g n) -> p g n", g=2)[:, :, 0:NCMP], 0.5)
            drained(nc.scalar.mul(v_cmp[0:NCMP, :, :], ps[0:NCMP, 64:64 + 2 * HD].rearrange("p (g n) -> p g n", g=2), 0.5), ("c2",))
            a.wait_ge(cmax, 1)
            act(pc[:, :, :, 0:NCMP], pc[:, :, :, 0:NCMP], ACT.Exp).then_inc(cexp, 1)

            def exps(h, t):
                n = (t + 1) * P
                o = 32 + 8 * (h % 2) + 4 * t
                a.wait_ge(neg_max, 2 * h + t + 1)
                if h >= 2:
                    wait_filled(a, ("pT", h - 2, t))
                ps = banks[bank_of[("s", h, t)][0]]
                act(prob[:, h % 2, t, 0:n], ps[:, 0:n], ACT.Exp, bias=stat[:, o:o + 1], accum_out=stat[:, o + 2:o + 3])
                drained(act(prob[:, h % 2, t, n:2 * n], ps[:, n:2 * n], ACT.Exp, bias=stat[:, o + 1:o + 2], accum_out=stat[:, o + 3:o + 4]), ("s", h, t))

            def evac_pT(h):
                ps = wait_filled(a, ("pT", h, 0))
                st.mark(cp(probT[:, h % 2, :, 0, 0:P], ps[:, 0:2 * P].rearrange("p (b q) -> p b q", b=2)))
                drained(cp(pcT[:, h % 2, :], ps[0:16, 2 * P:4 * P]), ("pT", h, 0))

            exps(0, 0)
            exps(0, 1)
            for h in range(HEADS):
                if h + 1 < HEADS:
                    exps(h + 1, 0)
                    exps(h + 1, 1)
                evac_pT(h)
                if h % 2 == 0 and h >= 2:
                    c = h // 2 - 1
                    ps = wait_filled(a, ("o", c))
                    drained(cp(oT[:, CC + c, :], ps[:, 0:S]), ("o", c))
                if h == 3:
                    ps = wait_filled(a, ("cvar",))
                    drained(cp(scr[:, 0, :], ps[:, 0:S]), ("cvar",))
                if h == 4:
                    for c in range(CC):
                        a.wait_ge(convn_ready, c + 1)
                        act(aT[:, c, PAD:PAD + S], oT[:, c, :], ACT.Tanh, scale=0.5).then_inc(convt_ready, 1)
            ps = wait_filled(a, ("o", CC - 1))
            drained(cp(oT[:, 2 * CC - 1, :], ps[:, 0:S]), ("o", CC - 1))

            for L in range(DEPTH):
                if L == 1:
                    for c in range(KC):
                        ps = wait_filled(a, ("odc", c))
                        if c >= 2:
                            wait_drained(a, ("odc", c - 2))
                        cp(scr[:, c % 2, :], ps[:, 0:S]).then_inc(od_c, 1)
                if L == 0:
                    a.wait_ge(small_loaded, 16 * 12)
                norm_act(a, 3 * L)
                for j in range(4):
                    ps = wait_filled(a, ("xq", L, j))
                    drained(cp(qxT[:, 2 * j:2 * j + 2, :], ps[:, :].rearrange("p (c s) -> p c s", c=2)), ("xq", L, j))

                def xexps(h):
                    o = 32 + 8 * (h % 2)
                    a.wait_ge(neg_max, 2 * HEADS + L * XH + h + 1)
                    if h >= 2:
                        wait_filled(a, ("xp", L, h - 2))
                    ps = banks[bank_of[("xs", L, h)][0]]
                    act(prob[:, h % 2, 0, 0:S], ps[:, 0:S], ACT.Exp, bias=stat[:, o:o + 1], accum_out=stat[:, o + 2:o + 3])
                    drained(act(prob[:, h % 2, 1, 0:S], ps[:, S:2 * S], ACT.Exp, bias=stat[:, o + 1:o + 2], accum_out=stat[:, o + 3:o + 4]), ("xs", L, h))

                def evac_xo(h):
                    ps = wait_filled(a, ("xo", L, h))
                    drained(cp(oT[:, 2 * h:2 * h + 2, :], ps[:, :].rearrange("p (c s) -> p c s", c=2)), ("xo", L, h))

                xexps(0)
                for h in range(XH):
                    if h + 1 < XH:
                        xexps(h + 1)
                    if h > 0:
                        evac_xo(h - 1)
                evac_xo(XH - 1)
                norm_act(a, 3 * L + 1)
                a.wait_ge(gexp_in, L + 1)
                for t in range(TT):
                    ins = act(esum[:, t, :], g8[:, t, 0:NG], ACT.Exp, bias=rs[:, 0, t:t + 1], accum_out=rs[:, 1, t:t + 1])
                    if t == 0:
                        st.mark(ins)
                ins.then_inc(gexp, 1)
                a.wait_ge(eexp_in, L + 1)
                act(rs[:, 3, :], rs[:, 2, :], ACT.Exp).then_inc(eexp, 1)

                def first_half(fam, n1):
                    a.wait_ge(fam.hid_done, n1)
                    act(th, banks[4][:, :], ACT.Tanh, scale=0.5).then_inc(fam.tanh_done, 1)

                def second_half(fam, n1, cb, yy, last=None):
                    a.wait_ge(fam.hidT_done, n1)
                    cp(hidT[:, :, :], banks[4][:, :].rearrange("p (c s) -> p c s", c=4)).then_inc(fam.hidT_ready, 1)
                    a.wait_ge(fam.comb_done, n1)
                    if last is not None:
                        a.wait_ge(fam.scattered, last)
                    cp(cb, banks[5][:, 0:S]).then_inc(fam.comb_ready, 1)
                    a.wait_ge(fam.y_done, n1)
                    for h in range(2):
                        ins = cp(yy[:, h * 512:(h + 1) * 512], banks[6 + h][:, :])
                    ins.then_inc(fam.y_ready, 1)

                g0 = L * (PAIRS + 1)
                a.wait_ge(rounds_ready, L + 1)
                with a.Fori(0, PAIRS) as i:
                    n1 = i + (L * PAIRS + 1)
                    first_half(main, n1)
                    second_half(main, n1, comb, y, i + (g0 + 1))
                    n, before = load_rounds(a, i)
                    with a.Fori(0, ROUNDS - 1) as q:
                        with a.If(n > q):
                            k1 = before + q + 1
                            first_half(over[L], k1)
                            second_half(over[L], k1, more_comb, more_y)
                if L + 1 < DEPTH:
                    norm_act(a, 3 * L + 2)

        @block.gpsimd
        def _(g):
            st = Steps(g, pool_step)
            ms, sel = nc.gpsimd.memset, nc.gpsimd.affine_select

            st.do(ms(ident[:, :], 0.0))
            sel(out=ident[:, :], in_=ident[:, :], compare_op=ALU.not_equal, fill=1.0, base=0,
                pattern=[[-1, P]], channel_multiplier=1).then_inc(consts_ready, 1)
            g.wait_ge(consts_ready, 1)
            def small(dst, src):
                g.dma_start(dst, src).then_inc(small_loaded, 16)

            small(w2c[:, 0, :, :], T["ev_cmp_w2_k"][0].rearrange("(h p) d -> p h d", p=P))
            small(w2c[:, 1, :, :], T["ev_cmp_w2_v"][0].rearrange("(h p) d -> p h d", p=P))
            for L in range(DEPTH):
                small(wr[:, L, :, 0:NG], T["moe_wg"][L].rearrange("(p k) g -> p k g", k=KC))
                small(wr[:, L, :, NG:NG + NE], T["moe_we"][L].rearrange("(p k) g e -> p k (g e)", k=KC))
            for m in range(2):
                for s, n in enumerate(("ln_mix", "ln_xa", "ln_ffn")):
                    dst = lngT[:, :, m, :].rearrange("p (l s) k -> p s l k", s=3)[:, s, :, :]
                    g.dma_start(dst, T[f"{n}_{'gb'[m]}"].rearrange("l (p k) -> p l k", k=KC)).then_inc(small_loaded, 16)
            g.dma_start(rbias[:, :, 0:NG], T["moe_bg"].unsqueeze(0).to_broadcast([P, DEPTH, NG])).then_inc(bias_loaded, 16)
            g.dma_start(rbias[:, :, NG:NG + NE], T["moe_be"].rearrange("l g e -> l (g e)").unsqueeze(0).to_broadcast([P, DEPTH, NE])).then_inc(bias_loaded, 16)
            ms(ones[:, :], 1.0)
            ms(onesc[:, :], 1.0 / CONV_CH)
            ms(zero16[:, :], 0.0)
            ms(half[:, :], -0.5)
            nc.gpsimd.iota(iota[:, :], pattern=[[1, CAP]], base=0, channel_multiplier=0, allow_small_or_imprecise_dtypes=True)
            for r_ in range(1, ROUNDS):
                ms(round_caps[:, r_ - 1:r_], float(r_ * CAP))
            ms(tri[:, :], 1.0)
            ms(causal[:, :], 0.0)
            ms(cmask[:, :, :], 1.0)
            st.do(ms(cbias[:, :, :], 0.0))
            sel(out=tri[:, :], in_=tri[:, :], compare_op=ALU.is_gt, fill=0.0, base=0, pattern=[[1, P]], channel_multiplier=-1)
            sel(out=causal[:, :], in_=causal[:, :], compare_op=ALU.is_ge, fill=NEG, base=0, pattern=[[-1, P]], channel_multiplier=1)
            pat = [[P, TT], [-CMP_STRIDE, 16]]
            sel(out=cmask[:, :, :], in_=cmask[:, :, :], compare_op=ALU.is_ge, fill=0.0, base=-31, pattern=pat, channel_multiplier=1)
            sel(out=cbias[:, :, :], in_=cbias[:, :, :], compare_op=ALU.is_ge, fill=NEG, base=-31, pattern=pat, channel_multiplier=1).then_inc(consts_ready, 1)

            def load_gb(i):
                n = ("ln_mix", "ln_xa", "ln_ffn")[i % 3]
                for m in range(2):
                    g.dma_start(gb[:, m, :], T[f"{n}_{'gb'[m]}"][i // 3:i // 3 + 1, :].to_broadcast([P, D])).then_inc(gb_loaded, 16)

            def norm(i):
                for t in range(TT):
                    g.wait_ge(ln_stats, 2 * i + t + 1)
                    st.do(nc.gpsimd.tensor_scalar(vare[:, t, :], mv[:, t, 1:2], EPS, None, ALU.add))
                    nc.gpsimd.tensor_tensor(rstd[:, t, :], vare[:, t, :], half[:, t:t + 1], ALU.pow).then_inc(ln_rstd, 1)

            wait_filled(g, (("mem",), 0, 1))
            wait_filled(g, (("mem",), 1, 1))
            load_gb(0)
            wait_drained(g, ("cvar",))
            st.do(nc.gpsimd.tensor_scalar(scr[:, 0, :], scr[:, 0, :], EPS, None, ALU.add))
            nc.gpsimd.tensor_tensor(scr[:, 1, :], scr[:, 0, :], half[:, :], ALU.pow).then_inc(stat_ready, 1)
            for i in range(LN_COUNT):
                norm(i)
                if i + 1 < LN_COUNT:
                    g.wait_ge(x_ready, 2 * i + 2)
                    load_gb(i + 1)


_OUTS = [((1, S, D), "float32")]


def kernel(**inputs):
    import numpy as _np
    import concourse.bacc as _bacc
    from concourse import mybir as _mybir
    from concourse.bass_utils import run_bass_kernel_spmd as _run

    nc = _bacc.Bacc("TRN2", target_bir_lowering=False, num_devices=1)
    arrays, tensors = {}, {}
    for name, value in inputs.items():
        a = _np.ascontiguousarray(value)
        arrays[f"in_{name}_dram"] = a
        tensors[name] = nc.dram_tensor(f"in_{name}_dram", a.shape, _mybir.dt.from_np(a.dtype), kind="ExternalInput").ap()
    shape, dtype = _OUTS[0]
    out = nc.dram_tensor("out_0_dram", shape, _mybir.dt.from_np(_np.dtype(dtype)), kind="ExternalOutput").ap()
    program(nc, tensors, out)
    r = _run(nc, [arrays], core_ids=[0])
    return r.results[0]["out_0_dram"]
```
